# Optimizing a Trainium2 kernel written in Bass

```python
import math
import jax, jax.numpy as jnp
from jax import lax
import numpy as np

D_MODEL = 1024
BATCH = 1
SEQ = 512
DEPTH = 1

BLOCK = 128
WINDOW = 128
H_A = 8
KV_A = 2
G_A = H_A // KV_A
DH_A = 64
H_B = 4
DH_B = 64
N_BUCKETS = 32
MAX_EXACT = N_BUCKETS // 2
REL_MAX_DIST = 128
N_BIAS_HEADS = H_A + H_B
N_EXPERTS = 32
TOP_K = 4
D_FF = D_MODEL
SWIGLU_ALPHA = 1.702
SWIGLU_LIMIT = 7.0
MOE_BLOCK = 128
NORM_EPS = 1e-6
SUBLN_EPS = 1e-5
QA_W = H_A * DH_A
KA_W = KV_A * DH_A
VA_W = KV_A * DH_A
QB_W = H_B * 2 * DH_B
KB_W = H_B * 2 * DH_B
VB_W = H_B * 2 * DH_B
SPLIT_SIZES = (QA_W, KA_W, VA_W, QB_W, KB_W, VB_W, D_MODEL, D_MODEL)
IN_W = QA_W + KA_W + VA_W + QB_W + KB_W + VB_W + 2 * D_MODEL
MIX_W = QA_W + H_B * 2 * DH_B

kernel_name = "hybrid_swa_sink_diffattn_moe_block"

def rms_norm(x, g, eps=NORM_EPS):
    xf = x.astype(jnp.float32)
    y = xf * lax.rsqrt(jnp.mean(xf * xf, axis=-1, keepdims=True) + eps)
    return (y * g.astype(jnp.float32)).astype(x.dtype)

def t5_bucket(dist):
    n = jnp.maximum(dist, 0)
    nf = jnp.maximum(n, 1).astype(jnp.float32)
    large = MAX_EXACT + (jnp.log(nf / MAX_EXACT) / math.log(REL_MAX_DIST / MAX_EXACT)
                         * (N_BUCKETS - MAX_EXACT)).astype(jnp.int32)
    large = jnp.minimum(large, N_BUCKETS - 1)
    return jnp.where(n < MAX_EXACT, n, large)

def sliding_window_attention(q, k, v, sinks, bias_table):
    b, s = q.shape[:2]
    nb = s // BLOCK
    qb = (q * DH_A ** -0.5).reshape(b, nb, BLOCK, KV_A, G_A, DH_A)

    def band(t):
        tp = jnp.pad(t, ((0, 0), (BLOCK, 0), (0, 0), (0, 0))).reshape(b, nb + 1, BLOCK, KV_A, DH_A)
        return jnp.concatenate([tp[:, :-1], tp[:, 1:]], axis=2)

    kb, vb = band(k), band(v)
    sc = jnp.einsum('bnqhgd,bnkhd->bnhgqk', qb, kb, preferred_element_type=jnp.float32)
    qi = jnp.arange(BLOCK)[:, None]
    kj = jnp.arange(2 * BLOCK)[None, :]
    dist = qi + BLOCK - kj
    bias = bias_table[t5_bucket(dist)].astype(jnp.float32)
    bias = bias.reshape(BLOCK, 2 * BLOCK, KV_A, G_A).transpose(2, 3, 0, 1)
    key_pos = jnp.arange(nb)[:, None, None] * BLOCK - BLOCK + kj[None]
    valid = (dist >= 0) & (dist < WINDOW) & (key_pos >= 0)
    sc = jnp.where(valid[None, :, None, None], sc + bias, -jnp.inf)
    sink = sinks.astype(jnp.float32).reshape(KV_A, G_A)[:, :, None, None]
    m = jnp.maximum(jnp.max(sc, axis=-1, keepdims=True), sink)
    e = jnp.exp(sc - m)
    p = e / (jnp.sum(e, axis=-1, keepdims=True) + jnp.exp(sink - m))
    o = jnp.einsum('bnhgqk,bnkhd->bnqhgd', p.astype(v.dtype), vb)
    return o.reshape(b, s, H_A * DH_A)

def differential_attention(q, k, v, lam, subln_g, lam_init, bias_table):
    b, s = q.shape[:2]
    nb = s // BLOCK
    qb = (q * DH_B ** -0.5).reshape(b, nb, BLOCK, H_B, 2, DH_B).transpose(1, 0, 3, 4, 2, 5)
    kt = k.transpose(0, 2, 3, 1, 4)
    vt = v.transpose(0, 2, 1, 3)
    k_pos = jnp.arange(s)

    def one_block(args):
        qblk, n = args
        sc = jnp.einsum('bhmqd,bhmkd->bhmqk', qblk, kt, preferred_element_type=jnp.float32)
        dist = n * BLOCK + jnp.arange(BLOCK)[:, None] - k_pos[None, :]
        bias = bias_table[t5_bucket(dist)].astype(jnp.float32).transpose(2, 0, 1)
        sc = jnp.where(dist >= 0, sc + bias[None, :, None], -jnp.inf)
        p = jax.nn.softmax(sc, axis=-1)
        a = p[:, :, 0] - lam * p[:, :, 1]
        return jnp.einsum('bhqk,bhkd->bhqd', a.astype(vt.dtype), vt)

    o = lax.map(one_block, (qb, jnp.arange(nb)))
    o = rms_norm(o, subln_g, SUBLN_EPS) * (1.0 - lam_init)
    return o.transpose(1, 0, 3, 2, 4).reshape(b, s, H_B * 2 * DH_B)

def clamped_swiglu(gu):
    gate = jnp.minimum(gu[..., :D_FF], SWIGLU_LIMIT)
    up = jnp.clip(gu[..., D_FF:], -SWIGLU_LIMIT, SWIGLU_LIMIT)
    return gate * jax.nn.sigmoid(SWIGLU_ALPHA * gate) * (up + 1.0)

def moe_ffn(h, w_router, b_router, w_gate_up, b_gate_up, w_down, b_down):
    b, s, d = h.shape
    t = b * s
    ht = h.reshape(t, d)
    logits = (ht @ w_router + b_router).astype(jnp.float32)
    top_val, top_idx = lax.top_k(logits, TOP_K)
    top_w = jax.nn.softmax(top_val, axis=-1)
    n_slots = t * TOP_K
    flat_e = top_idx.reshape(-1)
    order = jnp.argsort(flat_e).astype(jnp.int32)
    sorted_e = flat_e[order]
    counts = jnp.bincount(flat_e, length=N_EXPERTS).astype(jnp.int32)
    padded = (counts + MOE_BLOCK - 1) // MOE_BLOCK * MOE_BLOCK
    starts = jnp.cumsum(counts) - counts
    pends = jnp.cumsum(padded)
    pstarts = pends - padded
    dest = pstarts[sorted_e] + (jnp.arange(n_slots, dtype=jnp.int32) - starts[sorted_e])
    n_rows = n_slots + N_EXPERTS * MOE_BLOCK
    n_blocks = n_rows // MOE_BLOCK
    row_slot = jnp.full((n_rows,), n_slots, jnp.int32).at[dest].set(order)
    row_tok = row_slot // TOP_K
    row_w = jnp.concatenate([top_w.reshape(-1), jnp.zeros((1,), jnp.float32)])[row_slot]
    block_e = jnp.minimum(
        jnp.searchsorted(pends, jnp.arange(n_blocks, dtype=jnp.int32) * MOE_BLOCK, side='right'),
        N_EXPERTS - 1)
    xs = jnp.concatenate([ht, jnp.zeros((1, d), ht.dtype)])[row_tok].reshape(n_blocks, MOE_BLOCK, d)

    def expert_block(args):
        xb, e = args
        gu = xb @ w_gate_up[e] + b_gate_up[e]
        return clamped_swiglu(gu) @ w_down[e] + b_down[e]

    ys = lax.map(expert_block, (xs, block_e)).reshape(n_rows, d)
    ys = ys * row_w[:, None].astype(ys.dtype)
    out = jnp.zeros((t + 1, d), ys.dtype).at[row_tok].add(ys)[:t]
    return out.reshape(b, s, d)

def setup_inputs(seed: int = 0) -> dict:
    key = jax.random.key(seed)
    ks = jax.random.split(key, 22)
    nrm = jax.random.normal
    f32 = jnp.float32
    L, D, E, F = DEPTH, D_MODEL, N_EXPERTS, D_FF
    return {
        "x": nrm(ks[0], (BATCH, SEQ, D), f32),
        "c": nrm(ks[1], (BATCH, D), f32),
        "rel_bias_table": 0.2 * nrm(ks[2], (N_BUCKETS, N_BIAS_HEADS), f32),
        "w_ada": 0.5 * D ** -0.5 * nrm(ks[3], (L, D, 6 * D), f32),
        "b_ada": 0.01 * nrm(ks[4], (L, 6 * D), f32),
        "g_mix_pre": 1.0 + 0.05 * nrm(ks[5], (L, D), f32),
        "g_mix_post": 1.0 + 0.05 * nrm(ks[6], (L, D), f32),
        "g_ffn_pre": 1.0 + 0.05 * nrm(ks[7], (L, D), f32),
        "g_ffn_post": 1.0 + 0.05 * nrm(ks[8], (L, D), f32),
        "w_in": D ** -0.5 * nrm(ks[9], (L, D, IN_W), f32),
        "w_out": MIX_W ** -0.5 * nrm(ks[10], (L, MIX_W, D), f32),
        "attn_sinks": nrm(ks[11], (L, H_A), f32),
        "diff_lambda": 0.1 * nrm(ks[12], (L, 4, DH_B), f32),
        "diff_subln_g": 1.0 + 0.05 * nrm(ks[13], (L, 2 * DH_B), f32),
        "w_router": D ** -0.5 * nrm(ks[14], (L, D, E), f32),
        "b_router": 0.01 * nrm(ks[15], (L, E), f32),
        "w_gate_up": D ** -0.5 * nrm(ks[16], (L, E, D, 2 * F), f32),
        "b_gate_up": 0.01 * nrm(ks[17], (L, E, 2 * F), f32),
        "w_down": F ** -0.5 * nrm(ks[18], (L, E, F, D), f32),
        "b_down": 0.01 * nrm(ks[19], (L, E, D), f32),
    }

def reference(x, c, rel_bias_table, w_ada, b_ada, g_mix_pre, g_mix_post, g_ffn_pre, g_ffn_post,
              w_in, w_out, attn_sinks, diff_lambda, diff_subln_g, w_router, b_router,
              w_gate_up, b_gate_up, w_down, b_down):
    b, s, _ = x.shape
    split_idx = [int(v) for v in np.cumsum(SPLIT_SIZES)[:-1]]
    bias_a = rel_bias_table[:, :H_A]
    bias_b = rel_bias_table[:, H_A:]
    c_act = jax.nn.silu(c)
    for l in range(DEPTH):
        mod = (c_act @ w_ada[l] + b_ada[l])[:, None, :]
        sh_m, sc_m, gt_m, sh_f, sc_f, gt_f = jnp.split(mod, 6, axis=-1)

        h = rms_norm(x, g_mix_pre[l]) * (1.0 + sc_m) + sh_m
        proj = h @ w_in[l]
        qa, ka, va, qb, kb, vb, gza, gzb = jnp.split(proj, split_idx, axis=-1)
        o_a = sliding_window_attention(qa.reshape(b, s, H_A, DH_A), ka.reshape(b, s, KV_A, DH_A),
                                       va.reshape(b, s, KV_A, DH_A), attn_sinks[l], bias_a)
        lam_init = 0.8 - 0.6 * math.exp(-0.3 * l)
        lp = diff_lambda[l].astype(jnp.float32)
        lam = jnp.exp(jnp.sum(lp[0] * lp[1])) - jnp.exp(jnp.sum(lp[2] * lp[3])) + lam_init
        o_b = differential_attention(qb.reshape(b, s, H_B, 2, DH_B), kb.reshape(b, s, H_B, 2, DH_B),
                                     vb.reshape(b, s, H_B, 2 * DH_B), lam, diff_subln_g[l],
                                     lam_init, bias_b)
        y = (jax.nn.sigmoid(gza) * (o_a @ w_out[l][:QA_W])
             + jax.nn.sigmoid(gzb) * (o_b @ w_out[l][QA_W:]))
        x = x + gt_m * rms_norm(y, g_mix_post[l])

        h = rms_norm(x, g_ffn_pre[l]) * (1.0 + sc_f) + sh_f
        y = moe_ffn(h, w_router[l], b_router[l], w_gate_up[l], b_gate_up[l], w_down[l], b_down[l])
        x = x + gt_f * rms_norm(y, g_ffn_post[l])
    return x


_drawn_inputs = setup_inputs


def setup_inputs(seed=0):
    import zlib

    import numpy as np

    out = dict(_drawn_inputs(seed))
    spreads = {}
    factors = {'g_ffn_post': 4.284,
     'attn_sinks': 6.561,
     'b_router': 3.691,
     'b_gate_up': 8.0,
     'b_down': 8.0}
    for name, (base, spread) in spreads.items():
        noise = np.random.default_rng([zlib.crc32(name.encode()), seed]).standard_normal(out[name].shape)
        drawn = base * np.exp(spread * noise) if base else spread * noise
        out[name] = __import__('jax').numpy.asarray(drawn.astype(out[name].dtype))
    for name, factor in factors.items():
        out[name] = (out[name] * factor).astype(out[name].dtype)
    return out
```

```python
import math
from contextlib import ExitStack

import numpy as np

import concourse.bass as bass
from concourse import mybir

F32 = mybir.dt.float32
F32R = mybir.dt.float32r
BF16 = mybir.dt.bfloat16
I32 = mybir.dt.int32
U32 = mybir.dt.uint32
ALU = mybir.AluOpType
ACT = mybir.ActivationFunctionType
AX_X = mybir.AxisListType.X

P = 128
D = 1024
KC = D // P
T = 512
TC = T // P
H_A, KV_A, DH = 8, 2, 64
G_A = H_A // KV_A
H_B = 4
N_BUCKETS, MAX_EXACT, REL_MAX = 32, 16, 128
E = 32
TOPK = 4
FF = D
ALPHA, LIMIT = 1.702, 7.0
EPS, EPS_SUB = 1e-6, 1e-5
LAM_INIT = 0.8 - 0.6 * math.exp(0.0)
QK_SCALE = DH ** -0.5
MASKED = -1e30
PAD_ROW = 1 << 20
UN = 512
HK = KC // 2
NB = T // P
HALVES = 12
RAW, SPL = 6, 3
REL = 2 * P + P

C_QA, C_KA, C_QB = 0, H_A * DH, (H_A + 2 * KV_A) * DH


def bucket(dist):
    n = np.maximum(dist, 0)
    nf = np.maximum(n, 1).astype(np.float32)
    large = MAX_EXACT + (np.log(nf / MAX_EXACT) / math.log(REL_MAX / MAX_EXACT)
                         * (N_BUCKETS - MAX_EXACT)).astype(np.int32)
    return np.where(n < MAX_EXACT, n, np.minimum(large, N_BUCKETS - 1))


def constants():
    ident = np.eye(P, dtype=np.float32)
    upper = np.triu(np.ones((P, P), np.float32), 1)
    dist = 255 - np.arange(REL)
    hot = (bucket(dist)[None, :] == np.arange(N_BUCKETS)[:, None])
    near = (dist >= 0) & (dist < P)
    causal = dist >= 0
    oh = np.zeros((N_BUCKETS + 1, 2, REL), np.float32)
    oh[:N_BUCKETS, 0], oh[N_BUCKETS, 0] = hot * near, ~near
    oh[:N_BUCKETS, 1], oh[N_BUCKETS, 1] = hot * causal, ~causal
    sel = np.tile(np.eye(E, E + 1, dtype=np.float32), (3, 1))
    pick = np.concatenate([np.triu(np.ones((E, E + 2), np.float32), 2), np.eye(E, E + 2, 1, dtype=np.float32)], 1)
    iota_e = np.tile(np.arange(E, dtype=np.float32), (P, 1))
    tok = np.arange(TC)[None, :, None] * P + np.arange(P)[:, None, None]
    rows = (tok * TOPK + np.arange(TOPK)[None, None, :]).reshape(P, TC * TOPK).astype(np.int32)
    return ident, upper, oh.reshape(N_BUCKETS + 1, 2 * REL), sel, pick, iota_e, rows


def build(nc, x, c, rel_bias_table, w_ada, b_ada, g_mix_pre, g_mix_post, g_ffn_pre, g_ffn_post, w_in, w_out,
          attn_sinks, diff_lambda, diff_subln_g, w_router, b_router, w_gate_up, b_gate_up, w_down, b_down, out):
    ctx = ExitStack()
    with ctx:
        program(nc, ctx, x, c, rel_bias_table, w_ada, b_ada, g_mix_pre, g_mix_post, g_ffn_pre, g_ffn_post, w_in,
                w_out, attn_sinks, diff_lambda, diff_subln_g, w_router, b_router, w_gate_up, b_gate_up, w_down,
                b_down, out)


def program(nc, ctx, x, c, rel_bias_table, w_ada, b_ada, g_mix_pre, g_mix_post, g_ffn_pre, g_ffn_post, w_in, w_out,
            attn_sinks, diff_lambda, diff_subln_g, w_router, b_router, w_gate_up, b_gate_up, w_down, b_down, out):
    ident_c, upper_c, oh_c, sel_c, pick_c, iota_c, rows_c = [
        nc.inline_tensor(a, name=f"const_{n}").ap() for a, n in
        zip(constants(), ("ident", "upper", "buckets", "sel", "pick", "experts", "rows"))]

    def dram(name, shape, dt):
        return nc.dram_tensor(name, shape, dt, kind="Internal").ap()

    bias_d = dram("bias_vectors", (H_A + H_B, REL), F32)
    wide_d = dram("bias_vectors_repeated", (H_A + H_B, P, REL), F32)
    x1_d = dram("x_after_mixing", (T, D), F32)
    h2_d = dram("h_ffn", (T, D), F32)
    slot_d = dram("slot_rows", (T * E, 1), I32)
    y_d = dram("expert_rows", (T * TOPK, D), F32)

    base = 16512
    KB = 1024

    def at(name, shape, dt, off):
        return nc.alloc_sbuf_tensor_at(name, shape, dt, offset=base + off)

    raw = at("raw", [P, 4, HK, UN], F32, 0)
    whf = at("whf", [P, 2, HK, UN], F32R, 32 * KB)
    wlf = at("wlf", [P, 2, HK, UN], F32R, 48 * KB)
    hh = at("hh", [P, KC, T], F32R, 64 * KB)
    hl = at("hl", [P, KC, T], F32R, 80 * KB)
    s_sb = at("s_sb", [P, 2, 1024], F32, 0)
    pt = at("pt", [P, 2, 1024], F32, 8 * KB)
    ota = at("ota", [P, H_A // 2, T], F32, 16 * KB)
    otb = at("otb", [P, H_B, T], F32, 24 * KB)
    on = at("on", [P, H_B, P], F32, 32 * KB)
    osq = at("osq", [P, P], F32, 34 * KB)
    ball = at("ball", [96, 3 * D], F32, 52 * KB)
    wo = at("wo", [P, KC, D], F32, 64 * KB)
    y1 = at("y1", [P, 2, D], F32, 0)
    y2 = at("y2", [P, 2, D], F32, 8 * KB)
    x1s = at("x1s", [P, 2, D], F32, 36 * KB)
    h2s = at("h2s", [P, 2, D], F32, 44 * KB)
    h2t = at("h2t", [P, KC, P], F32, 52 * KB)
    junk = at("junk", [P, D], F32, 56 * KB)
    wr = at("wr", [P, KC, E], F32, 60 * KB)
    oneh = at("oneh", [P, TC * TOPK, E], F32, 0)
    ohr = at("ohr", [P, TC * TOPK, E], F32, 2 * KB)
    rawm = at("rawm", [P, RAW, HK, UN], F32, 0)
    wh = at("wh", [P, SPL, HK, UN], F32R, 48 * KB)
    wl = at("wl", [P, SPL, HK, UN], F32R, 72 * KB)
    yt = at("yt", [P, 2, TOPK, D], F32, 0)
    x1e = at("x1e", [P, 2, D], F32, 32 * KB)
    yo = at("yo", [P, 2, D], F32, 40 * KB)
    fin = at("fin", [P, 2, D], F32, 48 * KB)
    junke = at("junke", [P, D], F32, 56 * KB)

    qk = at("qk", [P, 12, T], F32, 96 * KB)
    ka2 = at("ka2", [P, KV_A, T], F32, 120 * KB)
    nat = at("nat", [P, TC, 5 * UN], F32, 124 * KB)
    gm = at("gm", [P, D], F32, 124 * KB)
    shm = at("shm", [P, D], F32, 128 * KB)
    gpre = at("gpre", [P, D], F32, 132 * KB)
    hnat = at("hnat", [P, 2, D], F32, 136 * KB)
    hx = at("hx", [P, 2, D], F32, 144 * KB)
    xsq = at("xsq", [P, D], F32, 152 * KB)
    xs = at("xs", [P, TC, D], F32, 164 * KB)
    va = at("va", [P, TC, P], F32, 164 * KB)
    toep = at("toep", [P, H_A + H_B, 2 * P], F32, 166 * KB)
    rv = at("rv", [H_A, 2, REL], F32, 166 * KB)
    oh = at("oh", [N_BUCKETS + 1, 2 * REL], F32, 178 * KB)
    acc = at("acc", [P, 6, D], F32, 181 * KB)
    grow1 = at("grow1", [P, D], F32, 181 * KB)
    grow2 = at("grow2", [P, D], F32, 185 * KB)
    gpm = at("gpm", [P, D], F32, 189 * KB)
    shf = at("shf", [P, D], F32, 193 * KB)
    gf = at("gf", [P, D], F32, 197 * KB)
    gpf = at("gpf", [P, D], F32, 201 * KB)
    grow3 = at("grow3", [P, D], F32, 44 * KB)
    xh = at("xh", [P, NB, KC, P], F32R, 96 * KB)
    xl = at("xl", [P, NB, KC, P], F32R, 112 * KB)
    ah = at("ah", [P, NB, KC, P], F32R, 128 * KB)
    al = at("al", [P, NB, KC, P], F32R, 144 * KB)
    xg0 = at("xg0", [P, D], F32, 160 * KB)
    y0 = at("y0", [P, D], F32, 164 * KB)
    xy = [None] + [at(f"xy{b}", [P, D], F32, (164 + 4 * b) * KB) for b in range(1, NB)]
    gsu = at("gsu", [P, 2 + NB - 1, 3, 256], F32, 186 * KB)
    bparts = at("bparts", [96, 3 * D], BF16, 180 * KB)

    small_at = [205 * KB]

    def small(name, shape, dt):
        n = int(np.prod(shape[1:])) * (2 if dt == BF16 else 4)
        t = at(name, shape, dt, small_at[0])
        small_at[0] += -(-n // 32) * 32
        assert base + small_at[0] <= 229344
        return t

    ident = small("ident", [P, P], F32)
    gtab = small("gtab", [P, NB, E + 2], I32)
    stab = small("stab", [P, NB, E + 2], I32)
    topw = small("topw", [P, TC * TOPK], F32)
    sel = small("sel", [96, E + 1], BF16)
    icur = small("icur", [P, 2, NB], I32)
    nk = small("nk", [1, 2 * (E + 2)], I32)
    one = small("one", [P, 1], F32)
    nhalf = small("nhalf", [P, H_B], F32)
    cact = small("cact", [P, KC], F32)
    sinkb = small("sinkb", [P, H_A], F32)
    nsink = small("nsink", [P, H_A], F32)
    farb = small("farb", [P, H_B], F32)
    subg = small("subg", [P, 1], F32)
    subgs = small("subgs", [P, 1], F32)
    nlam0 = small("nlam0", [P, 1], F32)
    nlam = small("nlam", [P, 1], F32)
    tabx = small("tabx", [N_BUCKETS + 1, H_A + H_B], F32)
    rs = small("rs", [P, 3, TC], F32)
    rs1 = small("rs1", [P, 3, TC], F32)
    ccol = at("ccol", [P, KC], F32, 156 * KB)
    csig = at("csig", [P, KC], F32, 156 * KB + 32)
    lp = at("lp", [P, 4, DH], F32, 157 * KB)
    lprod = at("lprod", [P, 2, DH], F32, 158 * KB)
    lsum = at("lsum", [P, 2], F32, 159 * KB)
    lexp = at("lexp", [P, 2], F32, 159 * KB + 32)
    st = at("st", [P, 2, 8, 4], F32, 35 * KB)
    NMX, MX, DSK, ESK, SUM, DEN, FAC = range(7)
    sn = at("sn", [P, 3, H_B], F32, 35 * KB + 256)

    r_at = [96 * KB]

    def route(name, shape, dt):
        n = int(np.prod(shape[1:])) * (2 if dt == BF16 else 4)
        t = at(name, shape, dt, r_at[0])
        r_at[0] += -(-n // 32) * 32
        assert r_at[0] <= 120 * KB
        return t

    lg = route("lg", [P, TC, E], F32)
    mv = route("mv", [P, TC, 8], F32)
    mi = route("mi", [P, TC, 8], U32)
    ef = route("ef", [P, TC, TOPK], F32)
    hot = route("hot", [P, TC, TOPK, E], F32)
    hotr = route("hotr", [P, TC, TOPK, E], F32)
    mask = route("mask", [P, TC, E], BF16)
    rsel = route("rsel", [P, TC * TOPK], F32)
    dest = route("dest", [P, TC * TOPK], I32)
    rows = route("rows", [P, TC * TOPK], I32)
    experts = route("experts", [P, E], F32)
    brow = route("brow", [P, E], F32)
    upperf = route("upperf", [P, P], F32)
    upper = route("upper", [P, P], BF16)
    onesb = route("onesb", [P, P], BF16)
    padt = route("padt", [P, P], I32)
    pick = route("pick", [E, 2 * (E + 2)], F32)
    over = route("over", [E, 4], F32)
    wexp = route("wexp", [P, TC, TOPK], F32)
    wsum = route("wsum", [P, 2, TC], F32)
    self_ = route("self", [96, E + 1], F32)
    begun = route("begun", [1, 2, E], F32)

    ps = ctx.enter_context(nc.psum_tensor("ps", [P, 8, UN], F32))

    def sem(name):
        return ctx.enter_context(nc.semaphore(name))

    c_in, x_in, gpre_in, small_in, bada_in = map(sem, ("c_in", "x_in", "gpre_in", "small_in", "bada_in"))
    oh_in, biasv_out, wide_out, toep_in, wo_in, ball_in, grow_in = map(
        sem, ("oh_in", "biasv_out", "wide_out", "toep_in", "wo_in", "ball_in", "grow_in"))
    raw_in = [sem(f"raw_in{s}") for s in range(4)]
    pool_set, one_set, csig_ready, cact_ready, ada_step, raw_used = map(
        sem, ("pool_set", "one_set", "csig_ready", "cact_ready", "ada_step", "raw_used"))
    lam_step, lexp_ready = sem("lam_step"), sem("lexp_ready")
    mod_ps, shm_ready, gm_ready = sem("mod_ps"), sem("shm_ready"), sem("gm_ready")
    xss_ready, xrs_step, hx_ready, h_ready, ht_ps, hh_ready, hl_ready = map(
        sem, ("xss_ready", "xrs_step", "hx_ready", "h_ready", "ht_ps", "hh_ready", "hl_ready"))
    wh_ready, half0_used, acc_done, evac_done = map(sem, ("wh_ready", "half0_used", "acc_done", "evac_done"))
    rv_ps, rv_ready, tab_ready = sem("rv_ps"), sem("rv_ready"), sem("tab_ready")
    latemod_ps, latemod_ready, shf_ready = sem("latemod_ps"), sem("latemod_ready"), sem("shf_ready")
    s_ps, s_ready, mx_step, exp_ready, den_step, p_ready, t_ps, pt_ready, o_ps, o_ready = map(
        sem, ("s_ps", "s_ready", "mx_step", "exp_ready", "den_step", "p_ready", "t_ps", "pt_ready", "o_ps",
              "o_ready"))
    osq_ready, sn_ready, on_ready, ot_ps, ot_ready = map(
        sem, ("osq_ready", "sn_ready", "on_ready", "ot_ps", "ot_ready"))
    sig_gates, ya_ps, yb_ps, y1_ready, y2_ready, y_ready, yss_ready, yrs_step, yg_ready, x1_ready = map(
        sem, ("sig_gates", "ya_ps", "yb_ps", "y1_ready", "y2_ready", "y_ready", "yss_ready", "yrs_step", "yg_ready",
              "x1_ready"))
    x1ss_ready, x1rs_step, h2x_ready, h2_ready, h2t_ps, h2t_ready, lg_ps, lg_ready = map(
        sem, ("x1ss_ready", "x1rs_step", "h2x_ready", "h2_ready", "h2t_ps", "h2t_ready", "lg_ps", "lg_ready"))
    x1_out, h2_out = [sem("x1_out0"), sem("x1_out1")], [sem("h2_out0"), sem("h2_out1")]
    xr_in = [sem("xr_in0"), sem("xr_in1")]
    route_in, slot_init, route_step, rank_ps, dest_ready, slot_out, slot_in, tab_done = map(
        sem, ("route_in", "slot_init", "route_step", "rank_ps", "dest_ready", "slot_out", "slot_in", "tab_done"))
    over_ready, nk_ps, nk_ready, wdiff_ready, wexp_ready = map(
        sem, ("over_ready", "nk_ps", "nk_ready", "wdiff_ready", "wexp_ready"))
    y_out = [sem("y_out_0"), sem("y_out_more")]
    junk_step, top_step, dest_step, wsum_step = map(sem, ("junk_step", "top_step", "dest_step", "wsum_step"))
    bias_step = sem("bias_step")

    def flat(ap):
        return ap.rearrange("p a b -> p (a b)")

    UNITS = [u for n in range(TC) for u in [("A", n, g) for g in range(KV_A)] + [("B", n, h) for h in range(H_B)]]
    N_T, N_N = 3, 5
    N_W = N_T + N_N
    N_SMALL = 9

    def win_half(col, h, n=UN):
        return w_in[0, h * HK * P:(h + 1) * HK * P, col].rearrange("(k p) n -> p k n", p=P)

    def bcast(src, n):
        return bass.AP(tensor=src.tensor, offset=src.offset, ap=[[0, P], [1, n]])


    def total(count, i):
        return sum(count(u) for u in UNITS[:i + 1])

    def n_scores(u):
        return 2 if u[0] == "B" and u[1] >= 2 else 1

    def n_max(u):
        return 3 if u[0] == "A" else 2

    def n_exp(u):
        return 5 if u[0] == "A" else 2

    def n_den(u):
        return 2 if u[0] == "A" else 3

    def n_a(i):
        return sum(u[0] == "A" for u in UNITS[:i + 1])

    def keys(u):
        return (max(u[1] - 1, 0) if u[0] == "A" else 0), u[1] + 1

    def scores_ps(i):
        w = 2 * (i % 2)
        if UNITS[i][0] == "A":
            lo = P if UNITS[i][1] == 0 else 0
            return ps[:, w:w + 2, :].rearrange("p a (b k) -> p (a b) k", b=2)[:, :, lo:2 * P]
        return ps[:, w:w + 2, :]

    def scores_sb(i):
        if UNITS[i][0] == "A":
            lo = P if UNITS[i][1] == 0 else 0
            return s_sb[:, i % 2, :].rearrange("p (a k) -> p a k", a=4)[:, :, lo:2 * P]
        return s_sb[:, i % 2, :].rearrange("p (m k) -> p m k", m=2)[:, :, 0:keys(UNITS[i])[1] * P]

    def attention_pe(pe):
        def scores(i):
            kind, n, g = UNITS[i]
            w = 2 * (i % 2)
            if i >= 2:
                pe.wait_ge(s_ready, total(n_scores, i - 2))
            if kind == "A":
                k0, k1 = keys(UNITS[i])
                for place in range(4):
                    a, b = place // 2, place % 2
                    lo = (place % 2) * 2 * P + (P if n == 0 else 0)
                    ins = nc.tensor.matmul(ps[:, w + a, lo:lo + (k1 - k0) * P],
                                           qk[64 * a:64 * a + 64, 2 * g + b, n * P:(n + 1) * P],
                                           ka2[64 * a:64 * a + 64, g, k0 * P:k1 * P], start=True, stop=True)
            else:
                for m in range(2):
                    ins = nc.tensor.matmul(ps[:, w + m, 0:(n + 1) * P], qk[64 * m:64 * m + 64, 4 + g, n * P:(n + 1) * P],
                                           qk[64 * m:64 * m + 64, 8 + g, 0:(n + 1) * P], start=True, stop=True)
            ins.then_inc(s_ps, 1)

        def transposed(i):
            kind, n, g = UNITS[i]
            pe.wait_ge(p_ready, i + 1)
            if i:
                pe.wait_ge(pt_ready, i)
            if kind == "A":
                for place in range(4):
                    for j in range(1 if n == 0 else 0, 2):
                        ins = nc.tensor.transpose(ps[:, 4 + place // 2, (place % 2 * 2 + j) * P:(place % 2 * 2 + j + 1) * P],
                                                  s_sb[:, i % 2, (2 * place + j) * P:(2 * place + j + 1) * P], ident[:])
            else:
                for j in range(n + 1):
                    ins = nc.tensor.transpose(ps[:, 4, j * P:(j + 1) * P], s_sb[:, i % 2, j * P:(j + 1) * P], ident[:])
            ins.then_inc(t_ps, 1)

        def values(i):
            kind, n, g = UNITS[i]
            pe.wait_ge(pt_ready, i + 1)
            if kind == "A":
                if n_a(i) > 1:
                    pe.wait_ge(o_ready, n_a(i) - 1)
                if n and g == 1:
                    pe.wait_ge(ot_ready, n)
                js = range(1 if n == 0 else 0, 2)
                for place in range(4):
                    a, b = place // 2, place % 2
                    for j in js:
                        ins = nc.tensor.matmul(ps[64 * a:64 * a + 64, 6, b * P:(b + 1) * P],
                                               va[:, n - 1 + j, 64 * g:64 * g + 64],
                                               pt[:, i % 2, (2 * place + j) * P:(2 * place + j + 1) * P],
                                               start=(j == js[0]), stop=(j == 1))
            else:
                if n and g == 0:
                    pe.wait_ge(on_ready, n)
                for j in range(n + 1):
                    ins = nc.tensor.matmul(ps[:, 7, g * P:(g + 1) * P], pt[:, i % 2, j * P:(j + 1) * P],
                                           nat[:, j, g * P:(g + 1) * P], start=(j == 0), stop=(j == n))
            ins.then_inc(o_ps, 1)

        def outputs_transposed(n):
            pe.wait_ge(on_ready, n + 1)
            pe.wait_ge(o_ready, min(2 * n + 3, 2 * TC))
            for h in range(H_B):
                ins = nc.tensor.transpose(ps[:, 6, h * P:(h + 1) * P], on[:, h, :], ident[:])
            ins.then_inc(ot_ps, 1)

        scores(0)
        for i in range(len(UNITS)):
            if i + 1 < len(UNITS):
                scores(i + 1)
            transposed(i)
            values(i)
            if i and UNITS[i - 1][0] == "B" and UNITS[i - 1][2] == H_B - 1:
                outputs_transposed(UNITS[i - 1][1])
        outputs_transposed(TC - 1)

    def attention_dve(dve):
        dve.wait_ge(toep_in, 16 * 5)

        def before(i):
            kind, n, g = UNITS[i]
            w = i % 2
            if i >= 2:
                dve.wait_ge(t_ps, i - 1)
            dve.wait_ge(s_ps, i + 1)
            src, dst = scores_ps(i), scores_sb(i)
            if kind == "A":
                lo = P if n == 0 else 0
                nc.vector.scalar_tensor_tensor(dst, src, QK_SCALE, toep[:, 4 * g:4 * g + 4, lo:2 * P], ALU.mult,
                                               ALU.add).then_inc(s_ready, 1)
                dve.wait_ge(s_ready, total(n_scores, i))
                nc.vector.tensor_reduce(st[:, w, MX, :], dst, AX_X, ALU.max).then_inc(mx_step, 1)
                dve.wait_ge(mx_step, total(n_max, i) - 2)
                nc.vector.scalar_tensor_tensor(st[:, w, NMX, :], st[:, w, MX, :], -1.0, nsink[:, 4 * g:4 * g + 4],
                                               ALU.mult, ALU.min).then_inc(mx_step, 1)
                dve.wait_ge(mx_step, total(n_max, i) - 1)
                nc.vector.tensor_tensor(st[:, w, DSK, :], st[:, w, NMX, :], sinkb[:, 4 * g:4 * g + 4],
                                        ALU.add).then_inc(mx_step, 1)
                return
            near = max(n - 1, 0) * P
            width = (n + 1) * P - near
            tile = toep[:, H_A + g:H_A + g + 1, 2 * P - width:2 * P].to_broadcast([P, 2, width])
            nc.vector.scalar_tensor_tensor(dst[:, :, near:near + width], src[:, :, near:near + width], QK_SCALE, tile,
                                           ALU.mult, ALU.add).then_inc(s_ready, 1)
            if near:
                nc.vector.tensor_scalar(dst[:, :, 0:near], src[:, :, 0:near], QK_SCALE, farb[:, g:g + 1], ALU.mult,
                                        ALU.add).then_inc(s_ready, 1)
            dve.wait_ge(s_ready, total(n_scores, i))
            nc.vector.tensor_reduce(st[:, w, MX, 0:2], dst, AX_X, ALU.max).then_inc(mx_step, 1)
            dve.wait_ge(mx_step, total(n_max, i) - 1)
            nc.vector.tensor_scalar(st[:, w, NMX, 0:2], st[:, w, MX, 0:2], -1.0, None, ALU.mult).then_inc(mx_step, 1)

        def after(i):
            kind, n, g = UNITS[i]
            w = i % 2
            dst = scores_sb(i)
            width = dst.shape[2]
            dve.wait_ge(exp_ready, total(n_exp, i))
            if kind == "A":
                nc.vector.tensor_tensor(st[:, w, DEN, :], st[:, w, SUM, :], st[:, w, ESK, :], ALU.add).then_inc(den_step, 1)
                dve.wait_ge(den_step, total(n_den, i) - 1)
                nc.vector.reciprocal(st[:, w, FAC, :], st[:, w, DEN, :]).then_inc(den_step, 1)
                dve.wait_ge(den_step, total(n_den, i))
                nc.vector.tensor_tensor(dst, dst, st[:, w, FAC, :].unsqueeze(2).to_broadcast([P, 4, width]),
                                        ALU.mult).then_inc(p_ready, 1)
                return
            nc.vector.reciprocal(st[:, w, FAC, 0:2], st[:, w, SUM, 0:2]).then_inc(den_step, 1)
            dve.wait_ge(den_step, total(n_den, i) - 2)
            nc.vector.tensor_tensor(st[:, w, DEN, 0:1], st[:, w, FAC, 1:2], nlam[:], ALU.mult).then_inc(den_step, 1)
            nc.vector.tensor_scalar(dst[:, 0, :], dst[:, 0, :], st[:, w, FAC, 0:1], None, ALU.mult).then_inc(den_step, 1)
            dve.wait_ge(den_step, total(n_den, i))
            nc.vector.scalar_tensor_tensor(dst[:, 0, :], dst[:, 1, :], st[:, w, DEN, 0:1], dst[:, 0, :], ALU.mult,
                                           ALU.add).then_inc(p_ready, 1)

        def sub_norm(n):
            dve.wait_ge(osq_ready, H_B * (n + 1))
            nc.vector.tensor_scalar(sn[:, 1, :], sn[:, 0, :], 1.0 / (2 * DH), EPS_SUB, ALU.mult,
                                    ALU.add).then_inc(sn_ready, 1)
            dve.wait_ge(sn_ready, 2 * n + 2)
            if n:
                dve.wait_ge(ot_ps, n)
            nc.vector.tensor_tensor(on[:], ps[:, 7, :].rearrange("p (h d) -> p h d", h=H_B),
                                    sn[:, 2, :].unsqueeze(2).to_broadcast([P, H_B, P]), ALU.mult).then_inc(on_ready, 1)

        before(0)
        for i in range(len(UNITS)):
            if i + 1 < len(UNITS):
                before(i + 1)
            if i and UNITS[i - 1][0] == "B" and UNITS[i - 1][2] == H_B - 1:
                sub_norm(UNITS[i - 1][1])
            after(i)
        sub_norm(TC - 1)

    def attention_act(act):
        def exps(i):
            kind, n, g = UNITS[i]
            w = i % 2
            dst = scores_sb(i)
            act.wait_ge(mx_step, total(n_max, i))
            for m in range(dst.shape[1]):
                nc.scalar.activation(dst[:, m, :], dst[:, m, :], ACT.Exp, bias=st[:, w, NMX, m:m + 1],
                                     accum_out=st[:, w, SUM, m:m + 1]).then_inc(exp_ready, 1)
            if kind == "A":
                nc.scalar.activation(st[:, w, ESK, :], st[:, w, DSK, :], ACT.Exp).then_inc(exp_ready, 1)

        def copies(i):
            kind, n, g = UNITS[i]
            act.wait_ge(t_ps, i + 1)
            if i >= 2:
                act.wait_ge(o_ps, i - 1)
            if kind == "A":
                lo = P if n == 0 else 0
                src = ps[:, 4:6, :].rearrange("p a (b k) -> p (a b) k", b=2)[:, :, lo:2 * P]
                dst = pt[:, i % 2, :].rearrange("p (a k) -> p a k", a=4)[:, :, lo:2 * P]
            else:
                src, dst = ps[:, 4, 0:(n + 1) * P], pt[:, i % 2, 0:(n + 1) * P]
            nc.scalar.activation(dst, src, ACT.Copy).then_inc(pt_ready, 1)
            act.wait_ge(o_ps, i + 1)
            if kind == "A":
                nc.scalar.activation(ota[:, 2 * g:2 * g + 2, n * P:(n + 1) * P],
                                     ps[:, 6, 0:2 * P].rearrange("p (a q) -> p a q", a=2), ACT.Copy).then_inc(o_ready, 1)
            elif g == H_B - 1:
                for h in range(H_B):
                    if n or h:
                        act.wait_ge(osq_ready, H_B * n + h)
                    nc.scalar.activation(osq[:], ps[:, 7, h * P:(h + 1) * P], ACT.Square,
                                         accum_out=sn[:, 0, h:h + 1]).then_inc(osq_ready, 1)

        def outputs_transposed(n):
            act.wait_ge(ot_ps, n + 1)
            nc.scalar.activation(otb[:, :, n * P:(n + 1) * P], ps[:, 6, :].rearrange("p (h q) -> p h q", h=H_B),
                                 ACT.Identity, scale=subgs[:, 0:1]).then_inc(ot_ready, 1)

        exps(0)
        for i in range(len(UNITS)):
            if i + 1 < len(UNITS):
                exps(i + 1)
            copies(i)
            if i and UNITS[i - 1][0] == "B" and UNITS[i - 1][2] == H_B - 1:
                outputs_transposed(UNITS[i - 1][1])
        outputs_transposed(TC - 1)

    def attention_pool(pool, power):
        pool.wait_ge(ball_in, 16 * 6)
        pool.wait_ge(latemod_ready, 3)
        nc.gpsimd.tensor_copy(bparts[:], ball[:]).then_inc(bias_step, 1)
        pool.wait_ge(bias_step, 1)
        for b in (1, 2):
            for lo in range(32 * b, 96, 32):
                nc.gpsimd.tensor_tensor(ball[lo:lo + 32, :], ball[lo:lo + 32, :], bparts[lo:lo + 32, :],
                                        ALU.subtract).then_inc(bias_step, 1)
            n = 3 if b == 1 else 6
            pool.wait_ge(bias_step, n)
            for lo in range(32 * b, 96, 32):
                nc.gpsimd.tensor_copy(bparts[lo:lo + 32, :], ball[lo:lo + 32, :]).then_inc(bias_step, 1)
            pool.wait_ge(bias_step, 5 if b == 1 else 7)
        for n in range(TC):
            power(sn[:, 2, :], sn[:, 1, :], sn_ready, 2 * n + 1)

    def merge_pe(pe):
        pe.wait_ge(wo_in, 32)

        def branches(t):
            pe.wait_ge(o_ready, 2 * (t + 1))
            pe.wait_ge(ot_ready, t + 1)
            if t == 0:
                pe.wait_ge(p_ready, len(UNITS))
            for b, (src, free, done) in enumerate(((ota, y1_ready, ya_ps), (otb, y2_ready, yb_ps))):
                if t:
                    pe.wait_ge(free, t)
                for half in range(2):
                    for k in range(4):
                        ins = nc.tensor.matmul(ps[:, 2 * b + half, :], src[:, k, t * P:(t + 1) * P],
                                               wo[:, 4 * b + k, half * UN:(half + 1) * UN], start=(k == 0), stop=(k == 3))
                ins.then_inc(done, 1)

        def router(t):
            pe.wait_ge(h2_ready, t + 1)
            if t == 0:
                pe.wait_ge(pt_ready, len(UNITS))
                pe.wait_ge(ot_ready, TC)
                pe.wait_ge(route_in, 16 * N_ROUTE)
            else:
                pe.wait_ge(h2t_ready, t)
            for k in range(KC):
                ins = nc.tensor.transpose(ps[:, 4 + k // 4, (k % 4) * P:(k % 4 + 1) * P],
                                          h2s[:, t % 2, k * P:(k + 1) * P], ident[:])
            ins.then_inc(h2t_ps, 1)
            pe.wait_ge(h2t_ready, t + 1)
            if t:
                pe.wait_ge(lg_ready, t)
            for k in range(KC):
                ins = nc.tensor.matmul(ps[:, 6, 0:E], h2t[:, k, :], wr[:, k, :], start=(k == 0), stop=(k == KC - 1))
            ins.then_inc(lg_ps, 1)

        branches(0)
        for t in range(TC):
            if t + 1 < TC:
                branches(t + 1)
            router(t)
        pe.wait_ge(route_step, MASKS_DONE)
        for t in range(TC):
            for s in range(t + 1):
                ins = nc.tensor.matmul(ps[:, 6, t * E:(t + 1) * E], upper[:] if s == t else onesb[:],
                                       mask[:, s, :], start=(s == 0), stop=(s == t))
        ins.then_inc(rank_ps, 1)
        for t in range(TC):
            ins = nc.tensor.matmul(ps[0:E, 7, 0:1], mask[:, t, :], onesb[:, 0:1], start=(t == 0), stop=(t == TC - 1))
        ins.then_inc(rank_ps, 1)
        pe.wait_ge(over_ready, 4)
        nc.tensor.matmul(ps[0:1, 5, 0:2 * (E + 2)], over[:, 3:4], pick[:], start=True, stop=True).then_inc(nk_ps, 1)

    MASKS_DONE = 6

    def merge_act(act):
        for t in range(TC):
            nc.scalar.activation(nat[:, t, UN:], nat[:, t, UN:], ACT.Sigmoid).then_inc(sig_gates, 1)
        n_junk = [0]

        def square(src, dst):
            if n_junk[0]:
                act.wait_ge(junk_step, n_junk[0])
            nc.scalar.activation(junk[:], src, ACT.Square, accum_out=dst).then_inc(junk_step, 1)
            n_junk[0] += 1

        for t in range(TC):
            act.wait_ge(y_ready, t + 1)
            square(y1[:, t % 2, :], rs[:, 0, t:t + 1])
            act.wait_ge(x1_ready, t + 1)
            square(x1s[:, t % 2, :], rs1[:, 0, t:t + 1])
            act.wait_ge(h2t_ps, t + 1)
            if t:
                act.wait_ge(lg_ps, t)
            nc.scalar.activation(flat(h2t[:]), flat(ps[:, 4:6, :]), ACT.Copy).then_inc(h2t_ready, 1)
        act.wait_ge(wdiff_ready, 1)
        nc.scalar.activation(wexp[:], wexp[:], ACT.Exp).then_inc(wexp_ready, 1)

    def merge_dve(dve):
        for t in range(TC):
            w = t % 2
            dve.wait_ge(sig_gates, t + 1)
            dve.wait_ge(ya_ps, t + 1)
            nc.vector.tensor_tensor(y1[:, w, :].rearrange("p (a b) -> p a b", a=2), ps[:, 0:2, :],
                                    nat[:, t, UN:UN + D].rearrange("p (a b) -> p a b", a=2), ALU.mult).then_inc(y1_ready, 1)
            dve.wait_ge(yb_ps, t + 1)
            nc.vector.tensor_tensor(y2[:, w, :].rearrange("p (a b) -> p a b", a=2), ps[:, 2:4, :],
                                    nat[:, t, UN + D:].rearrange("p (a b) -> p a b", a=2), ALU.mult).then_inc(y2_ready, 1)
            dve.wait_ge(y1_ready, t + 1)
            dve.wait_ge(y2_ready, t + 1)
            nc.vector.tensor_tensor(y1[:, w, :], y1[:, w, :], y2[:, w, :], ALU.add).then_inc(y_ready, 1)
            dve.wait_ge(junk_step, 2 * t + 1)
            nc.vector.tensor_scalar(rs[:, 1, t:t + 1], rs[:, 0, t:t + 1], 1.0 / D, EPS, ALU.mult,
                                    ALU.add).then_inc(yrs_step, 1)
            dve.wait_ge(yrs_step, 2 * t + 2)
            dve.wait_ge(y_ready, t + 1)
            nc.vector.scalar_tensor_tensor(y2[:, w, :], y1[:, w, :], rs[:, 2, t:t + 1], gpm[:], ALU.mult,
                                           ALU.mult).then_inc(yg_ready, 1)
            dve.wait_ge(yg_ready, t + 1)
            dve.wait_ge(xr_in[w], 16 * (t // 2 + 1))
            nc.vector.tensor_tensor(x1s[:, w, :], x1s[:, w, :], y2[:, w, :], ALU.add).then_inc(x1_ready, 1)
            dve.wait_ge(junk_step, 2 * t + 2)
            nc.vector.tensor_scalar(rs1[:, 1, t:t + 1], rs1[:, 0, t:t + 1], 1.0 / D, EPS, ALU.mult,
                                    ALU.add).then_inc(x1rs_step, 1)
            dve.wait_ge(x1rs_step, 2 * t + 2)
            dve.wait_ge(x1_ready, t + 1)
            nc.vector.scalar_tensor_tensor(y1[:, w, :], x1s[:, w, :], rs1[:, 2, t:t + 1], gf[:], ALU.mult,
                                           ALU.mult).then_inc(h2x_ready, 1)
            dve.wait_ge(h2x_ready, t + 1)
            if t >= 2:
                dve.wait_ge(h2_out[w], 16 * (t // 2))
                dve.wait_ge(h2t_ps, t - 1)
            nc.vector.tensor_tensor(h2s[:, w, :], y1[:, w, :], shf[:], ALU.add).then_inc(h2_ready, 1)
            dve.wait_ge(lg_ps, t + 1)
            nc.vector.tensor_tensor(lg[:, t, :], ps[:, 6, 0:E], brow[:], ALU.add).then_inc(lg_ready, 1)
        dve.wait_ge(lg_ready, TC)
        for t in range(TC):
            nc.vector.max(mv[:, t, :], lg[:, t, :]).then_inc(top_step, 1)
        dve.wait_ge(top_step, TC)
        for t in range(TC):
            nc.vector.max_index(mi[:, t, :], mv[:, t, :], lg[:, t, :]).then_inc(top_step, 1)
        dve.wait_ge(top_step, 2 * TC)
        nc.vector.tensor_copy(ef[:], mi[:, :, 0:TOPK]).then_inc(route_step, 1)
        nc.vector.tensor_copy(upper[:], upperf[:]).then_inc(route_step, 1)
        nc.vector.memset(onesb[:], 1.0).then_inc(route_step, 1)
        nc.vector.tensor_copy(sel[:], self_[:]).then_inc(route_step, 1)
        dve.wait_ge(route_step, 4)
        hotf = hot[:].rearrange("p t j e -> p (t j) e")
        hotrf = hotr[:].rearrange("p t j e -> p (t j) e")
        eff = ef[:].rearrange("p t j -> p (t j)")
        nc.vector.tensor_tensor(hotf, experts[:].unsqueeze(1).to_broadcast([P, TC * TOPK, E]),
                                eff.unsqueeze(2).to_broadcast([P, TC * TOPK, E]), ALU.is_equal).then_inc(route_step, 1)
        dve.wait_ge(route_step, 5)
        with nc.allow_low_precision(reason="sums of 0 and 1 that are 0 or 1"):
            nc.vector.tensor_reduce(mask[:], hot[:].rearrange("p t j e -> p t e j"), AX_X,
                                    ALU.add).then_inc(route_step, 1)
        nc.vector.tensor_tensor(wexp[:], mv[:, :, 0:TOPK], mv[:, :, 0:1].to_broadcast([P, TC, TOPK]),
                                ALU.subtract).then_inc(wdiff_ready, 1)
        dve.wait_ge(rank_ps, 1)
        nc.vector.tensor_tensor(hotr[:], hot[:],
                                ps[:, 6, 0:TC * E].rearrange("p (t e) -> p t e", t=TC).unsqueeze(2).to_broadcast(
                                    [P, TC, TOPK, E]), ALU.mult).then_inc(dest_step, 1)
        dve.wait_ge(dest_step, 1)
        nc.vector.tensor_reduce(rsel[:], hotrf, AX_X, ALU.add).then_inc(dest_step, 1)
        dve.wait_ge(dest_step, 2)
        nc.vector.scalar_tensor_tensor(dest[:], rsel[:], float(E), eff, ALU.mult, ALU.add).then_inc(dest_ready, 1)
        dve.wait_ge(rank_ps, 2)
        for b in range(NB - 1):
            nc.vector.tensor_scalar(over[:, b:b + 1], ps[0:E, 7, 0:1], (b + 1) * P + 0.5, None,
                                    ALU.is_gt).then_inc(over_ready, 1)
        dve.wait_ge(over_ready, NB - 1)
        nc.vector.tensor_reduce(over[:, 3:4], over[:, 0:3], AX_X, ALU.add).then_inc(over_ready, 1)
        dve.wait_ge(nk_ps, 1)
        nc.vector.tensor_copy(nk[:], ps[0:1, 5, 0:2 * (E + 2)]).then_inc(nk_ready, 1)
        dve.wait_ge(wexp_ready, 1)
        nc.vector.tensor_reduce(wsum[:, 0, :], wexp[:], AX_X, ALU.add).then_inc(wsum_step, 1)
        dve.wait_ge(wsum_step, 1)
        nc.vector.reciprocal(wsum[:, 1, :], wsum[:, 0, :]).then_inc(wsum_step, 1)
        dve.wait_ge(wsum_step, 2)
        nc.vector.tensor_tensor(topw[:].rearrange("p (t j) -> p t j", t=TC), wexp[:],
                                wsum[:, 1, :].unsqueeze(2).to_broadcast([P, TC, TOPK]), ALU.mult).then_inc(wsum_step, 1)
        dve.wait_ge(slot_in, 16)
        nc.vector.tensor_scalar(gtab[:], stab[:], 2, None, ALU.arith_shift_right).then_inc(tab_done, 1)

    N_ROUTE = 7

    def merge_pool(pool, power):
        pool.wait_ge(pt_ready, len(UNITS))
        pool.dma_start(wr[:], w_router[0].rearrange("(k p) e -> p k e", p=P)).then_inc(route_in, 16)
        pool.dma_start(brow[:], bcast(b_router[0], E)).then_inc(route_in, 16)
        pool.dma_start(upperf[:], upper_c).then_inc(route_in, 16)
        pool.dma_start(experts[:], iota_c).then_inc(route_in, 16)
        pool.dma_start(rows[:], rows_c).then_inc(route_in, 16)
        pool.dma_start(pick[:], pick_c).then_inc(route_in, 16)
        pool.dma_start(self_[:], sel_c).then_inc(route_in, 16)
        for m in range(2):
            pool.dma_start(begun[0:1, m, :], iota_c[0:1, :]).then_inc(y_out[m], 16)
        nc.gpsimd.memset(padt[:], PAD_ROW).then_inc(pool_set, 1)
        nc.gpsimd.memset(stab[:], PAD_ROW).then_inc(pool_set, 1)
        pool.wait_ge(pool_set, 3)
        pool.dma_start(slot_d.rearrange("(p a) b -> p (a b)", p=P), padt[:]).then_inc(slot_init, 16)
        for t in range(TC):
            power(rs[:, 2, t:t + 1], rs[:, 1, t:t + 1], yrs_step, 2 * t + 1)
            power(rs1[:, 2, t:t + 1], rs1[:, 1, t:t + 1], x1rs_step, 2 * t + 1)
        pool.wait_ge(dest_ready, 1)
        pool.wait_ge(slot_init, 16)
        for i in range(TC * TOPK):
            pool.indirect_dma_start(out=slot_d, out_offset=bass.IndirectOffsetOnAxis(ap=dest[:, i:i + 1], axis=0),
                                    in_=rows[:, i:i + 1], in_offset=None).then_inc(slot_out, 16)
        pool.wait_ge(slot_out, 16 * TC * TOPK)
        pool.dma_start(stab[:, :, 1:E + 1], slot_d.rearrange("(b p e) a -> p b (e a)", b=NB, p=P)).then_inc(slot_in, 16)

    def merge_sync(sp):
        for t in range(2):
            sp.wait_ge(on_ready, TC)
            sp.dma_start(x1s[:, t, :], x[0, t * P:(t + 1) * P, :]).then_inc(xr_in[t], 16)
        for t in range(TC):
            w = t % 2
            sp.wait_ge(x1_ready, t + 1)
            sp.dma_start(x1_d[t * P:(t + 1) * P, :], x1s[:, w, :]).then_inc(x1_out[w], 16)
            sp.wait_ge(h2_ready, t + 1)
            sp.dma_start(h2_d[t * P:(t + 1) * P, :], h2s[:, w, :]).then_inc(h2_out[w], 16)
            if t < 2:
                sp.wait_ge(x1_out[w], 16)
                sp.dma_start(x1s[:, w, :], x[0, (t + 2) * P:(t + 3) * P, :]).then_inc(xr_in[w], 16)

    half_used, acc_more, wh_done, wl_done = map(sem, ("half_used", "acc_more", "wh_done", "wl_done"))
    rawm_in = [sem(f"rawm_in{s}") for s in range(RAW)]
    pair = lambda name: (sem(name + "_0"), sem(name + "_more"))
    xg_in, xt_done, xh_done, xl_done, gcur, scur = map(pair, ("xg_in", "xt_done", "xh_done", "xl_done", "gcur", "scur"))
    g_ready, acc_free, up_ready, s_done, act_ready, at_done, ah_done, al_done, y_copied = map(
        pair, ("g_ready", "acc_free", "up_ready", "s_done", "act_ready", "at_done", "ah_done", "al_done", "y_copied"))
    y_half_copied = [sem("y_half_copied0"), y_copied[0]]
    pool_passed = sem("pool_passed")
    START = 1
    from_one = [s for p in (xt_done, xh_done, xl_done, gcur, scur, g_ready, acc_free, up_ready, s_done, act_ready,
                            at_done, ah_done, al_done, y_copied, (y_half_copied[0], acc_more)) for s in p]
    T_GU, U_ALL = 4, 6

    class Expert:

        def __init__(self, eng, e):
            self.eng, self.e = eng, e
            self.before = eng.value_load(nk[0:1, bass.ds(e + 1, 1)], min_val=0, max_val=T * TOPK // P)
            self.more = eng.value_load(nk[0:1, bass.ds(e + (E + 3), 1)], min_val=0, max_val=NB - 1)

        def count(self, steps, step, b):
            if b == 0:
                return self.e * steps + step + 1 + START
            return self.before * steps + self.more * step + b + START

        def all_more(self, steps, step):
            return self.before * steps + self.more * (step + 1) + START

        def earlier(self, steps, b):
            return (self.before if b else self.e) * steps + START

        def stored(self, b):
            return ((self.before if b else self.e) + START) * 16

        def blocks(self, work):
            with self.eng.If(self.more >= 1):
                work(1)
                for b in range(2, NB):
                    with self.eng.If(self.more >= b):
                        work(b)
            work(0)

    def weights(e, v):
        rows = slice(v % 2 * HK * P, (v % 2 + 1) * HK * P)
        if v < 2 * T_GU:
            t = v // 2
            return [w_gate_up[0, bass.ds(e, 1), rows, up * FF + 256 * t:up * FF + 256 * (t + 1)].rearrange(
                "a (k p) n -> p (a k) n", p=P) for up in range(2)]
        t = v // 2 - T_GU
        return [w_down[0, bass.ds(e, 1), rows, UN * t:UN * (t + 1)].rearrange("a (k p) n -> p (a k) n", p=P)]

    def slot_bytes(v):
        one_of = lambda x: 32 if x < 2 * T_GU else 16
        return one_of(v) if v < RAW else one_of(v - RAW) + one_of(v)

    def experts_sync(sp):
        sp.wait_ge(h2t_ps, TC)
        for w in range(2):
            sp.wait_ge(x1_out[w], 32)
            sp.wait_ge(h2_out[w], 32)

        def load(e, v):
            for n, src in enumerate(weights(e, v)):
                dst = rawm[:, v % RAW, :, :] if v >= 2 * T_GU else rawm[:, v % RAW, :, 256 * n:256 * (n + 1)]
                sp.dma_start(dst, src).then_inc(rawm_in[v % RAW], 16)

        for v in range(RAW):
            load(0, v)

        def rest(e, ahead):
            for v in range(RAW, HALVES + (RAW if ahead else 0)):
                sp.wait_ge(wl_done, e * HALVES + (v - RAW + 1))
                load(e + v // HALVES, v % HALVES)

        with sp.Fori(0, E - 1) as e:
            rest(e, True)
        rest(E - 1, False)

    def experts_pe(pe):
        pe.wait_ge(nk_ready, 1)

        def tokens_transposed(x):
            def work(b):
                m = min(b, 1)
                if b:
                    pe.wait_ge(xg_in[1], (x.before + x.more) * 16)
                    pe.wait_ge(xl_done[1], x.count(1, 0, b) - 1)
                else:
                    pe.wait_ge(xg_in[0], (x.e + 1) * 16)
                    pe.wait_ge(xl_done[1], x.all_more(1, 0))
                pe.wait_ge(xl_done[0], x.earlier(1, 0))
                src = xy[b] if b else xg0
                for k in range(KC):
                    ins = nc.tensor.transpose(ps[:, 5 + k // 4, (k % 4) * P:(k % 4 + 1) * P], src[:, k * P:(k + 1) * P],
                                              ident[:])
                ins.then_inc(xt_done[m], 1)
            x.blocks(work)

        def act_transposed(x, t):
            def work(b):
                m = min(b, 1)
                pe.wait_ge(act_ready[m], x.count(T_GU, t, b))
                pe.wait_ge(al_done[0], x.e * T_GU + t + START)
                pe.wait_ge(al_done[1], x.count(T_GU, t, b) - 1 if b else x.all_more(T_GU, t))
                for j in range(2):
                    ins = nc.tensor.transpose(ps[:, 7, j * P:(j + 1) * P],
                                              gsu[:, 1 + b if b else t % 2, 2, j * P:(j + 1) * P], ident[:])
                ins.then_inc(at_done[m], 1)
            x.blocks(work)

        def half(x, v):
            u, h = v // 2, v % 2
            pe.wait_ge(wl_done, x.e * HALVES + (v + 1))

            def work(b):
                bank = 1 + b if b else u % 2
                dst = ps[:, bank, :]
                if v == 0:
                    pe.wait_ge(xl_done[min(b, 1)], x.all_more(1, 0) if b else x.count(1, 0, 0))
                if v == 8 or v == 9:
                    tiles = 2 if v == 8 else 4
                    pe.wait_ge(al_done[min(b, 1)], x.all_more(T_GU, tiles - 1) if b else x.count(T_GU, tiles - 1, 0))
                if h == 0:
                    if b == 0:
                        if u <= 1:
                            pe.wait_ge(y_half_copied[u], x.earlier(1, 0))
                        else:
                            pe.wait_ge(acc_free[0], x.count(T_GU, u - 2, 0))
                    elif u == 0:
                        pe.wait_ge(y_copied[1], x.earlier(2, 1))
                    elif u <= T_GU:
                        pe.wait_ge(acc_free[1], x.count(T_GU, u - 1, b))
                    else:
                        pe.wait_ge(y_copied[1], x.count(2, 0, b))
                    if u < T_GU:
                        bias = bparts[:, 0:2 * D].rearrange("p (a n) -> p a n", a=2)[:, :, 256 * u:256 * (u + 1)]
                    else:
                        bias = bparts[:, 2 * D + UN * (u - T_GU):2 * D + UN * (u - T_GU + 1)]
                    nc.tensor.matmul(dst, sel[:, bass.ds(x.e, 1)].to_broadcast([96, P]), bias, start=True, stop=False)
                a_h, a_l = (xh, xl) if u < T_GU else (ah, al)
                for k in range(HK):
                    kk = HK * h + k
                    nc.tensor.matmul(dst, a_h[:, b, kk, :], wh[:, v % SPL, k, :], start=False, stop=False)
                    nc.tensor.matmul(dst, a_h[:, b, kk, :], wl[:, v % SPL, k, :], start=False, stop=False)
                    ins = nc.tensor.matmul(dst, a_l[:, b, kk, :], wh[:, v % SPL, k, :], start=False, stop=kk == KC - 1)
                if b == 0:
                    ins.then_inc(half_used, 1)
                elif h:
                    ins.then_inc(acc_more, 1)
            x.blocks(work)

        tokens_transposed(Expert(pe, 0))
        pe.wait_ge(nk_ready, 1)
        with pe.Fori(0, E) as e:
            x = Expert(pe, e)
            for v in range(9):
                half(x, v)
                if v in (3, 5, 7):
                    act_transposed(x, (v - 3) // 2)
            act_transposed(x, 3)
            tokens_transposed(Expert(pe, e + 1))
            for v in range(9, HALVES):
                half(x, v)

    def experts_act(act):
        act.wait_ge(nk_ready, 1)

        def split_high(x, v, used=None):
            act.wait_ge(rawm_in[v % RAW], x.e * slot_bytes(v % RAW + RAW) + slot_bytes(v))
            if used is not None:
                act.wait_ge(half_used, used)
            nc.scalar.activation(flat(wh[:, v % SPL, :, :]), flat(rawm[:, v % RAW, :, :]), ACT.Copy).then_inc(wh_done, 1)

        def tokens_high(x):
            def work(b):
                m = min(b, 1)
                act.wait_ge(xt_done[m], x.count(1, 0, b))
                nc.scalar.activation(flat(xh[:, b, :, :]), flat(ps[:, 5:7, :]), ACT.Copy).then_inc(xh_done[m], 1)
            x.blocks(work)

        def sigmoid(x, t):
            def work(b):
                m, s = min(b, 1), (1 + b if b else t % 2)
                act.wait_ge(g_ready[m], x.count(T_GU, t, b))
                nc.scalar.activation(gsu[:, s, 1, :], gsu[:, s, 0, :], ACT.Sigmoid, scale=ALPHA).then_inc(s_done[m], 1)
            x.blocks(work)

        def act_high(x, t):
            def work(b):
                m = min(b, 1)
                act.wait_ge(at_done[m], x.count(T_GU, t, b))
                nc.scalar.activation(flat(ah[:, b, 2 * t:2 * t + 2, :]), ps[:, 7, 0:2 * P], ACT.Copy).then_inc(ah_done[m], 1)
            x.blocks(work)

        def outputs(x, d, after):
            def work(b):
                m = min(b, 1)
                if b:
                    act.wait_ge(acc_more, x.count(U_ALL, T_GU + d, b))
                    act.wait_ge(xt_done[1], after.all_more(1, 0))
                    act.wait_ge(y_out[1], x.stored(1))
                else:
                    act.wait_ge(half_used, x.e * HALVES + (10 + 2 * d))
                    act.wait_ge(y_out[0], x.stored(0))
                dst = xy[b] if b else y0
                nc.scalar.activation(dst[:, d * UN:(d + 1) * UN], ps[:, 1 + b if b else d, :],
                                     ACT.Copy).then_inc(y_copied[1] if b else y_half_copied[d], 1)
            x.blocks(work)

        def middle(x):
            def split(v):
                split_high(x, v, x.e * HALVES + (v - SPL + 1))
            split(3)
            split(4)
            sigmoid(x, 0)
            split(5)
            split(6)
            act_high(x, 0)
            sigmoid(x, 1)
            split(7)
            split(8)
            act_high(x, 1)
            sigmoid(x, 2)
            split(9)
            split(10)
            act_high(x, 2)
            sigmoid(x, 3)
            act_high(x, 3)
            split(11)

        first = Expert(act, 0)
        tokens_high(first)
        for v in range(SPL):
            split_high(first, v)
        with act.Fori(0, E - 1) as e:
            x = Expert(act, e)
            middle(x)
            after = Expert(act, e + 1)
            tokens_high(after)
            split_high(after, 0, e * HALVES + (HALVES - SPL + 1))
            outputs(x, 0, after)
            split_high(after, 1, e * HALVES + (HALVES - SPL + 2))
            split_high(after, 2, e * HALVES + (HALVES - SPL + 3))
            outputs(x, 1, after)
        last, end = Expert(act, E - 1), Expert(act, E)
        middle(last)
        tokens_high(end)
        outputs(last, 0, end)
        outputs(last, 1, end)

    def experts_dve(dve):
        def split_low(x, v):
            dve.wait_ge(wh_done, x.e * HALVES + (v + 1))
            nc.vector.tensor_tensor(flat(wl[:, v % SPL, :, :]), flat(rawm[:, v % RAW, :, :]), flat(wh[:, v % SPL, :, :]),
                                    ALU.subtract).then_inc(wl_done, 1)

        def tokens_low(x):
            def work(b):
                m = min(b, 1)
                dve.wait_ge(xh_done[m], x.count(1, 0, b))
                nc.vector.tensor_tensor(flat(xl[:, b, :, :]), flat(ps[:, 5:7, :]), flat(xh[:, b, :, :]),
                                        ALU.subtract).then_inc(xl_done[m], 1)
            x.blocks(work)

        def act_low(x, t):
            def work(b):
                m = min(b, 1)
                dve.wait_ge(ah_done[m], x.count(T_GU, t, b))
                nc.vector.tensor_tensor(flat(al[:, b, 2 * t:2 * t + 2, :]), ps[:, 7, 0:2 * P],
                                        flat(ah[:, b, 2 * t:2 * t + 2, :]), ALU.subtract).then_inc(al_done[m], 1)
            x.blocks(work)

        def gate_up(x, t):
            def work(b):
                m, s = min(b, 1), (1 + b if b else t % 2)
                bank = 1 + b if b else t % 2
                if b:
                    dve.wait_ge(acc_more, x.count(U_ALL, t, b))
                    if t:
                        dve.wait_ge(at_done[1], x.count(T_GU, t - 1, b))
                else:
                    dve.wait_ge(half_used, x.e * HALVES + (2 * t + 2))
                nc.vector.tensor_scalar(gsu[:, s, 0, :], ps[:, bank, 0:256], LIMIT, None, ALU.min).then_inc(g_ready[m], 1)
                nc.vector.tensor_scalar(gsu[:, s, 2, :], ps[:, bank, 256:512], LIMIT, -LIMIT, ALU.min,
                                        ALU.max).then_inc(acc_free[m], 1)
                dve.wait_ge(g_ready[m], x.count(T_GU, t, b))
                dve.wait_ge(acc_free[m], x.count(T_GU, t, b))
                nc.vector.scalar_tensor_tensor(gsu[:, s, 2, :], gsu[:, s, 2, :], 1.0, gsu[:, s, 0, :], ALU.add,
                                               ALU.mult).then_inc(up_ready[m], 1)
            x.blocks(work)

        dve.wait_ge(nk_ready, 1)
        tokens_low(Expert(dve, 0))
        with dve.Fori(0, E) as e:
            x = Expert(dve, e)
            for v in range(4):
                split_low(x, v)
            gate_up(x, 0)
            split_low(x, 4)
            split_low(x, 5)
            gate_up(x, 1)
            split_low(x, 6)
            act_low(x, 0)
            split_low(x, 7)
            gate_up(x, 2)
            split_low(x, 8)
            act_low(x, 1)
            split_low(x, 9)
            gate_up(x, 3)
            split_low(x, 10)
            act_low(x, 2)
            act_low(x, 3)
            split_low(x, 11)
            tokens_low(Expert(dve, e + 1))

    def experts_pool(pool):
        pool.wait_ge(h2_ready, TC)
        pool.wait_ge(lg_ready, TC)
        nc.gpsimd.memset(xg0[:], 0.0).then_inc(pool_set, 1)
        for b in range(1, NB):
            nc.gpsimd.memset(xy[b][:], 0.0).then_inc(pool_set, 1)
        pool.wait_ge(pool_set, 3 + NB)
        pool.wait_ge(tab_done, 1)
        pool.wait_ge(nk_ready, 1)
        for w in range(2):
            pool.wait_ge(h2_out[w], 32)

        def gather(x, done):
            def work(b):
                m = min(b, 1)
                if b:
                    pool.wait_ge(xt_done[1], x.earlier(1, 1))
                    pool.wait_ge(y_out[1], done.stored(1))
                else:
                    pool.wait_ge(xt_done[0], x.earlier(1, 0))
                pool.sem_inc(pool_passed, 1)
                nc.gpsimd.tensor_copy(icur[:, 0, b:b + 1], gtab[:, b, bass.ds(x.e + 1, 1)]).then_inc(gcur[m], 1)
                pool.wait_ge(gcur[m], x.count(1, 0, b))
                pool.sem_inc(pool_passed, 1)
                pool.indirect_dma_start(out=(xy[b] if b else xg0)[:], out_offset=None, in_=h2_d,
                                        in_offset=bass.IndirectOffsetOnAxis(ap=icur[:, 0, b:b + 1], axis=0),
                                        bounds_check=T - 1, oob_is_err=False).then_inc(xg_in[m], 16)
            x.blocks(work)

        def scatter(x):
            def work(b):
                m = min(b, 1)
                if b:
                    pool.wait_ge(y_copied[1], x.all_more(2, 1))
                    pool.wait_ge(y_out[1], x.stored(1))
                else:
                    for half in y_half_copied:
                        pool.wait_ge(half, x.count(1, 0, 0))
                    pool.wait_ge(y_out[0], x.stored(0))
                pool.sem_inc(pool_passed, 1)
                nc.gpsimd.tensor_copy(icur[:, 1, b:b + 1], stab[:, b, bass.ds(x.e + 1, 1)]).then_inc(scur[m], 1)
                pool.wait_ge(scur[m], x.count(1, 0, b))
                pool.sem_inc(pool_passed, 1)
                pool.indirect_dma_start(out=y_d, out_offset=bass.IndirectOffsetOnAxis(ap=icur[:, 1, b:b + 1], axis=0),
                                        in_=(xy[b] if b else y0)[:], in_offset=None, bounds_check=T * TOPK - 1,
                                        oob_is_err=False).then_inc(y_out[m], 16)
            x.blocks(work)

        def activation(x, t):
            def work(b):
                m, s = min(b, 1), (1 + b if b else t % 2)
                pool.wait_ge(s_done[m], x.count(T_GU, t, b))
                pool.wait_ge(up_ready[m], x.count(T_GU, t, b))
                nc.gpsimd.tensor_tensor(gsu[:, s, 2, :], gsu[:, s, 2, :], gsu[:, s, 1, :], ALU.mult).then_inc(act_ready[m], 1)
            x.blocks(work)

        first = Expert(pool, 0)
        gather(first, first)
        with pool.Fori(0, E) as e:
            x = Expert(pool, e)
            gather(Expert(pool, e + 1), x)
            for t in range(T_GU):
                activation(x, t)
            scatter(x)

    fin_out = [sem("fin_out0"), sem("fin_out1")]
    yt_in, x1e_in = [sem("yt_in0"), sem("yt_in1")], [sem("x1e_in0"), sem("x1e_in1")]
    comb_step, fsq_ready, frs_step, fg_ready, fin_ready = map(
        sem, ("comb_step", "fsq_ready", "frs_step", "fg_ready", "fin_ready"))

    def final_pool(pool, power):
        end = Expert(pool, E)
        pool.wait_ge(y_out[0], 16 * (E + START))
        pool.wait_ge(y_out[1], end.stored(1))
        pool.sem_inc(pool_passed, 1)
        rows_of = y_d.rearrange("(t p j) d -> t p j d", p=P, j=TOPK)
        for t in range(TC):
            w = t % 2
            if t >= 2:
                pool.wait_ge(fin_ready, t - 1)
            pool.dma_start(yt[:, w, :, :], rows_of[t]).then_inc(yt_in[w], 16)
            pool.dma_start(x1e[:, w, :], x1_d[t * P:(t + 1) * P, :]).then_inc(x1e_in[w], 16)
            if t:
                power(rs1[:, 2, t - 1:t], rs1[:, 1, t - 1:t], frs_step, 2 * t - 1)
        power(rs1[:, 2, TC - 1:TC], rs1[:, 1, TC - 1:TC], frs_step, 2 * TC - 1)

    def final_dve(dve):
        for t in range(TC):
            w = t % 2
            dve.wait_ge(yt_in[w], 16 * (t // 2 + 1))
            for j in range(TOPK):
                wgt = topw[:, t * TOPK + j:t * TOPK + j + 1]
                if j == 0:
                    ins = nc.vector.tensor_scalar(yo[:, w, :], yt[:, w, j, :], wgt, None, ALU.mult)
                else:
                    dve.wait_ge(comb_step, t * TOPK + j)
                    ins = nc.vector.scalar_tensor_tensor(yo[:, w, :], yt[:, w, j, :], wgt, yo[:, w, :], ALU.mult, ALU.add)
                ins.then_inc(comb_step, 1)
            dve.wait_ge(fsq_ready, t + 1)
            nc.vector.tensor_scalar(rs1[:, 1, t:t + 1], rs1[:, 0, t:t + 1], 1.0 / D, EPS, ALU.mult,
                                    ALU.add).then_inc(frs_step, 1)
            dve.wait_ge(frs_step, 2 * t + 2)
            dve.wait_ge(comb_step, (t + 1) * TOPK)
            nc.vector.scalar_tensor_tensor(yo[:, w, :], yo[:, w, :], rs1[:, 2, t:t + 1], gpf[:], ALU.mult,
                                           ALU.mult).then_inc(fg_ready, 1)
            dve.wait_ge(fg_ready, t + 1)
            dve.wait_ge(x1e_in[w], 16 * (t // 2 + 1))
            if t >= 2:
                dve.wait_ge(fin_out[w], 16)
            nc.vector.tensor_tensor(fin[:, w, :], x1e[:, w, :], yo[:, w, :], ALU.add).then_inc(fin_ready, 1)

    def final_act(act):
        for t in range(TC):
            act.wait_ge(comb_step, (t + 1) * TOPK)
            if t:
                act.wait_ge(fsq_ready, t)
            nc.scalar.activation(junke[:], yo[:, t % 2, :], ACT.Square, accum_out=rs1[:, 0, t:t + 1]).then_inc(fsq_ready, 1)

    def final_sync(sp):
        for t in range(TC):
            w = t % 2
            sp.wait_ge(fin_ready, t + 1)
            sp.dma_start(out[0, t * P:(t + 1) * P, :], fin[:, w, :]).then_inc(fin_out[w], 16)
        for w in range(2):
            sp.wait_ge(fin_out[w], 32)
    block = ctx.enter_context(nc.Block())

    @block.sync
    def _(sp):
        def load(slot, g, src, n=UN):
            if not isinstance(g, int) or g >= 4:
                sp.wait_ge(raw_used, g - 3)
            sp.dma_start(raw[:, slot, :, 0:n], src).then_inc(raw_in[slot], 16)

        def ada(col, h):
            return w_ada[0, h * HK * P:(h + 1) * HK * P, col].rearrange("(k p) n -> p k n", p=P)

        for g in range(8):
            load(g % 4, g, ada(bass.ds(g // 2 * UN, UN), g % 2))
        load(0, 8, win_half(bass.ds(C_KA, 256), 0), 256)
        load(1, 9, win_half(bass.ds(C_KA, 256), 1), 256)
        load(2, 10, win_half(bass.ds(C_QA, UN), 0))
        load(3, 11, win_half(bass.ds(C_QA, UN), 1))
        load(0, 12, ada(bass.ds(4 * UN, UN), 0))
        load(1, 13, win_half(bass.ds(C_QB, UN), 0))
        load(2, 14, ada(bass.ds(4 * UN, UN), 1))
        with sp.Fori(1, N_W - 1) as u:
            load(3, 11 + 4 * u, win_half(bass.ds(C_QB + (u - 1) * UN, UN), 1))
            load(0, 12 + 4 * u, ada(bass.ds((4 + u) * UN, UN), 0))
            load(1, 13 + 4 * u, win_half(bass.ds(C_QB + u * UN, UN), 0))
            load(2, 14 + 4 * u, ada(bass.ds((4 + u) * UN, UN), 1))
        g = 11 + 4 * (N_W - 1)
        load(3, g, win_half(bass.ds(C_QB + (N_W - 2) * UN, UN), 1))
        load(0, g + 1, ada(bass.ds(11 * UN, UN), 0))
        load(1, g + 2, ada(bass.ds(11 * UN, UN), 1))
        sp.wait_ge(acc_done, 5 + 4 * N_W)
        for k in range(2):
            sp.dma_start(wo[:, 4 * k:4 * k + 4, :],
                         w_out[0, 4 * k * P:4 * (k + 1) * P, :].rearrange("(k p) n -> p k n", p=P)).then_inc(wo_in, 16)
        merge_sync(sp)
        experts_sync(sp)
        final_sync(sp)

    @block.scalar
    def _(act):
        act.dma_start(ccol[:], c[0, :].rearrange("(k p) -> p k", p=P), allow_slow_non_contiguous=True).then_inc(c_in, 16)
        act.dma_start(xs[:], x[0].rearrange("(c p) d -> p c d", p=P)).then_inc(x_in, 16)
        act.dma_start(gpre[:], bcast(g_mix_pre[0], D)).then_inc(gpre_in, 16)
        act.wait_ge(c_in, 16)
        nc.scalar.activation(csig[:], ccol[:], ACT.Sigmoid).then_inc(csig_ready, 1)
        act.wait_ge(lam_step, 2)
        nc.scalar.activation(lexp[:], lsum[:], ACT.Exp).then_inc(lexp_ready, 1)
        act.wait_ge(x_in, 16)
        for t in range(TC):
            if t:
                act.wait_ge(xss_ready, t)
            nc.scalar.activation(xsq[:], xs[:, t, :], ACT.Square, accum_out=rs[:, 0, t:t + 1]).then_inc(xss_ready, 1)
        act.wait_ge(mod_ps, 1)
        nc.scalar.activation(shm[:], flat(ps[:, 0:2, :]), ACT.Copy).then_inc(shm_ready, 1)
        for t in range(TC):
            act.wait_ge(ht_ps, t + 1)
            b = 4 + 2 * (t % 2)
            nc.scalar.activation(hh[:, :, t * P:(t + 1) * P], ps[:, b:b + 2, :].rearrange("p a (b c) -> p (a b) c", c=P),
                                 ACT.Copy).then_inc(hh_ready, 1)

        def split_high(m, slot, m_slot, arrivals, n=UN):
            act.wait_ge(raw_in[slot], 16 * arrivals)
            nc.scalar.activation(whf[:, m_slot, :, 0:n], raw[:, slot, :, 0:n], ACT.Copy).then_inc(wh_ready, 1)

        split_high(0, 0, 0, 3, 256)
        split_high(1, 1, 1, 3, 256)
        act.wait_ge(half0_used, 1)
        split_high(2, 2, 0, 3)
        act.wait_ge(acc_done, 1)
        for g in range(KV_A):
            for half in range(2):
                nc.scalar.activation(ka2[64 * half:64 * half + 64, g, :], ps[64 * g:64 * g + 64, 4, :],
                                     ACT.Copy).then_inc(evac_done, 1)
        for t in range(TC):
            act.wait_ge(acc_done, 2 + t)
            nc.scalar.activation(va[:, t, :], ps[:, t, 0:P], ACT.Copy).then_inc(evac_done, 1)

        def unit(u, dst, last=False):
            act.wait_ge(acc_done, 5 + 4 * u)
            split_high(3 + 2 * u, 3, 1, 3 + u)
            if not last:
                act.wait_ge(half0_used, 2 + u)
                split_high(4 + 2 * u, 1, 0, 4 + u)
            for k in range(4):
                act.wait_ge(acc_done, 5 + 4 * u + k + 1)
                nc.scalar.activation(dst(u, k), ps[:, k, :], ACT.Copy).then_inc(evac_done, 1)

        def to_qk(u, k):
            return qk[:, bass.ds(4 * u + k, 1), :].rearrange("p a n -> p (a n)")

        def to_nat(u, k):
            return nat[:, k, bass.ds((u - N_T) * UN, UN)]

        with act.Fori(0, N_T) as u:
            unit(u, to_qk)
        with act.Fori(N_T, N_W - 1) as u:
            unit(u, to_nat)
        unit(N_W - 1, to_nat, last=True)
        act.wait_ge(latemod_ps, 2)
        nc.scalar.activation(shf[:], flat(ps[:, 2:4, :]), ACT.Copy).then_inc(shf_ready, 1)
        attention_act(act)
        merge_act(act)
        experts_act(act)
        final_act(act)


    @block.tensor
    def _(pe):
        on_all = one[:, 0:1].to_broadcast([P, P])
        accf = acc[:].rearrange("p a b -> p (a b)")

        def spread(j, bank, signal=None):
            ins = nc.tensor.matmul(ps[:, bank, :], on_all, accf[:, j * UN:(j + 1) * UN], start=True, stop=True)
            if signal is not None:
                ins.then_inc(signal, 1)

        for s in from_one:
            pe.sem_inc(s, START)
        pe.wait_ge(one_set, 1)
        pe.wait_ge(raw_used, 8)
        for j in range(4):
            spread(j, j, mod_ps if j % 2 else None)
        pe.wait_ge(small_in, 16 * N_SMALL)
        for t in range(TC):
            pe.wait_ge(h_ready, t + 1)
            if t >= 2:
                pe.wait_ge(hl_ready, t - 1)
            for k in range(KC):
                ins = nc.tensor.transpose(ps[:, 4 + 2 * (t % 2) + k // 4, (k % 4) * P:(k % 4 + 1) * P],
                                          hnat[:, t % 2, k * P:(k + 1) * P], ident[:])
            ins.then_inc(ht_ps, 1)
        pe.wait_ge(hl_ready, TC)

        def three(dst, a_h, a_l, b_h, b_l, first, last):
            nc.tensor.matmul(dst, a_h, b_h, start=first, stop=False)
            nc.tensor.matmul(dst, a_h, b_l, start=False, stop=False)
            return nc.tensor.matmul(dst, a_l, b_h, start=False, stop=last)

        for h in range(2):
            pe.wait_ge(raw_used, 9 + h)
            for k in range(HK):
                kk = HK * h + k
                ins = three(ps[:, 4, :], whf[:, h, k, 0:P], wlf[:, h, k, 0:P], hh[:, kk, :], hl[:, kk, :],
                            kk == 0, kk == KC - 1)
            if h:
                ins.then_inc(acc_done, 1)
            for t in range(TC):
                for k in range(HK):
                    kk = HK * h + k
                    ins = three(ps[:, t, 0:P], hh[:, kk, t * P:(t + 1) * P], hl[:, kk, t * P:(t + 1) * P],
                                whf[:, h, k, P:2 * P], wlf[:, h, k, P:2 * P], kk == 0, kk == KC - 1)
                if h:
                    ins.then_inc(acc_done, 1)
            if h == 0:
                ins.then_inc(half0_used, 1)
        pe.wait_ge(tab_ready, 1)
        pe.wait_ge(oh_in, 16)
        nc.tensor.matmul(ps[0:H_A, 6, 0:REL], tabx[:, 0:H_A], oh[:, 0:REL], start=True, stop=True).then_inc(rv_ps, 1)
        nc.tensor.matmul(ps[0:H_B, 7, 0:REL], tabx[:, H_A:H_A + H_B], oh[:, REL:2 * REL], start=True,
                         stop=True).then_inc(rv_ps, 1)

        def unit(u, transposed):
            for h in range(2):
                pe.wait_ge(raw_used, (10 if h == 0 else 12) + 4 * u)
                for q in range(4):
                    if h == 0:
                        pe.wait_ge(evac_done, 5 + 4 * u + q)
                    for k in range(HK):
                        kk = HK * h + k
                        if transposed:
                            ins = three(ps[:, q, :], whf[:, h, k, q * P:(q + 1) * P], wlf[:, h, k, q * P:(q + 1) * P],
                                        hh[:, kk, :], hl[:, kk, :], kk == 0, kk == KC - 1)
                        else:
                            ins = three(ps[:, q, :], hh[:, kk, q * P:(q + 1) * P], hl[:, kk, q * P:(q + 1) * P],
                                        whf[:, h, k, :], wlf[:, h, k, :], kk == 0, kk == KC - 1)
                    if h:
                        ins.then_inc(acc_done, 1)
                if h == 0:
                    ins.then_inc(half0_used, 1)

        pe.wait_ge(raw_used, 11)
        with pe.Fori(0, N_T) as u:
            unit(u, True)
        with pe.Fori(N_T, N_W) as u:
            unit(u, False)
        pe.wait_ge(raw_used, 42)
        pe.wait_ge(evac_done, 8 + 4 * N_W)
        pe.wait_ge(rv_ready, 2)
        for j in range(4, 12):
            spread(j, j - 4, latemod_ps if j % 2 else None)
        pe.wait_ge(latemod_ready, 3)
        pe.wait_ge(shf_ready, 1)
        attention_pe(pe)
        merge_pe(pe)
        experts_pe(pe)

    @block.vector
    def _(dve):
        accf = acc[:].rearrange("p a b -> p (a b)")
        nc.vector.memset(one[:], 1.0).then_inc(one_set, 1)
        nc.vector.memset(nhalf[:], -0.5).then_inc(one_set, 1)
        nc.vector.memset(tabx[N_BUCKETS:N_BUCKETS + 1, :], MASKED).then_inc(tab_ready, 1)
        dve.wait_ge(c_in, 16)
        dve.wait_ge(csig_ready, 1)
        nc.vector.tensor_tensor(cact[:], ccol[:], csig[:], ALU.mult).then_inc(cact_ready, 1)
        dve.wait_ge(small_in, 16 * N_SMALL)
        nc.vector.tensor_tensor(lprod[:], lp[:, 0::2, :], lp[:, 1::2, :], ALU.mult).then_inc(lam_step, 1)
        dve.wait_ge(lam_step, 1)
        nc.vector.tensor_reduce(lsum[:], lprod[:], AX_X, ALU.add).then_inc(lam_step, 1)
        nc.vector.tensor_scalar(subgs[:], subg[:], 1.0 - LAM_INIT, None, ALU.mult).then_inc(lam_step, 1)
        nc.vector.tensor_scalar(nsink[:], sinkb[:], -1.0, None, ALU.mult).then_inc(lam_step, 1)
        dve.wait_ge(lexp_ready, 1)
        nc.vector.tensor_scalar(nlam0[:], lexp[:, 1:2], -LAM_INIT, None, ALU.add).then_inc(lam_step, 1)
        dve.wait_ge(lam_step, 5)
        nc.vector.tensor_tensor(nlam[:], nlam0[:], lexp[:, 0:1], ALU.subtract).then_inc(lam_step, 1)
        dve.wait_ge(bada_in, 16)
        dve.wait_ge(cact_ready, 1)

        def ada(a, h, slot, arrivals, g, last_g):
            dve.wait_ge(raw_in[slot], 16 * arrivals)
            dst = accf[:, bass.ds(a * UN, UN)]
            for k in range(HK):
                if k == 0 and h:
                    dve.wait_ge(raw_used, last_g + 1)
                elif k:
                    dve.wait_ge(ada_step, 3 * (2 * a + h) + k)
                ins = nc.vector.scalar_tensor_tensor(dst, raw[:, slot, k, :], cact[:, HK * h + k:HK * h + k + 1], dst,
                                                     ALU.mult, ALU.add)
                ins.then_inc(raw_used if k == HK - 1 else ada_step, 1)

        for g in range(8):
            ada(g // 2, g % 2, g % 4, g // 4 + 1, g, g - 1)
            if g == 1:
                dve.wait_ge(xss_ready, TC)
                nc.vector.tensor_scalar(rs[:, 1, :], rs[:, 0, :], 1.0 / D, EPS, ALU.mult, ALU.add).then_inc(xrs_step, 1)
        dve.wait_ge(gpre_in, 16)
        dve.wait_ge(mod_ps, 2)
        nc.vector.scalar_tensor_tensor(gm[:].rearrange("p (a b) -> p a b", a=2), ps[:, 2:4, :], 1.0,
                                       gpre[:].rearrange("p (a b) -> p a b", a=2), ALU.add,
                                       ALU.mult).then_inc(gm_ready, 1)
        dve.wait_ge(gm_ready, 1)
        dve.wait_ge(xrs_step, 2)
        dve.wait_ge(shm_ready, 1)
        dve.wait_ge(x_in, 16)

        def h_low(t):
            dve.wait_ge(hh_ready, t + 1)
            b = 4 + 2 * (t % 2)
            nc.vector.tensor_tensor(hl[:, :, t * P:(t + 1) * P], ps[:, b:b + 2, :].rearrange("p a (b c) -> p (a b) c", c=P),
                                    hh[:, :, t * P:(t + 1) * P], ALU.subtract).then_inc(hl_ready, 1)

        for t in range(TC):
            nc.vector.scalar_tensor_tensor(hx[:, t % 2, :], xs[:, t, :], rs[:, 2, t:t + 1], gm[:], ALU.mult,
                                           ALU.mult).then_inc(hx_ready, 1)
            dve.wait_ge(hx_ready, t + 1)
            if t >= 2:
                dve.wait_ge(ht_ps, t - 1)
            nc.vector.tensor_tensor(hnat[:, t % 2, :], hx[:, t % 2, :], shm[:], ALU.add).then_inc(h_ready, 1)
            if t:
                h_low(t - 1)
        h_low(TC - 1)

        def split_low(m, slot, m_slot, n=UN):
            dve.wait_ge(wh_ready, m + 1)
            nc.vector.tensor_tensor(wlf[:, m_slot, :, 0:n], raw[:, slot, :, 0:n], whf[:, m_slot, :, 0:n],
                                    ALU.subtract).then_inc(raw_used, 1)

        split_low(0, 0, 0, 256)
        split_low(1, 1, 1, 256)
        split_low(2, 2, 0)
        for b in range(2):
            n = (H_A, H_B)[b]
            dve.wait_ge(rv_ps, b + 1)
            nc.vector.tensor_copy(rv[0:n, b, :], ps[0:n, 6 + b, 0:REL]).then_inc(rv_ready, 1)

        def unit(u, last=False):
            split_low(3 + 2 * u, 3, 1)
            ada(4 + u, 0, 0, 4 + u, 12 + 4 * u, None)
            if not last:
                split_low(4 + 2 * u, 1, 0)
                ada(4 + u, 1, 2, 4 + u, 14 + 4 * u, 12 + 4 * u)
            else:
                ada(4 + u, 1, 1, 4 + u, 13 + 4 * u, 12 + 4 * u)

        with dve.Fori(0, N_W - 1) as u:
            unit(u)
        unit(N_W - 1, last=True)

        def halves(t):
            return t.rearrange("p (a b) -> p a b", a=2)

        dve.wait_ge(grow_in, 48)
        dve.wait_ge(latemod_ps, 1)
        nc.vector.tensor_tensor(halves(gpm[:]), ps[:, 0:2, :], halves(grow1[:]), ALU.mult).then_inc(latemod_ready, 1)
        dve.wait_ge(latemod_ps, 3)
        nc.vector.scalar_tensor_tensor(halves(gf[:]), ps[:, 4:6, :], 1.0, halves(grow2[:]), ALU.add,
                                       ALU.mult).then_inc(latemod_ready, 1)
        dve.wait_ge(latemod_ps, 4)
        nc.vector.tensor_tensor(halves(gpf[:]), ps[:, 6:8, :], halves(grow3[:]), ALU.mult).then_inc(latemod_ready, 1)
        attention_dve(dve)
        merge_dve(dve)
        experts_dve(dve)
        final_dve(dve)

    @block.gpsimd
    def _(pool):
        nc.gpsimd.memset(acc[:], 0.0).then_inc(pool_set, 1)
        pool.dma_start(ident[:], ident_c).then_inc(small_in, 16)
        pool.dma_start(tabx[0:N_BUCKETS, :], rel_bias_table).then_inc(small_in, 16)
        for g in range(KV_A):
            for a in range(2):
                src = bass.AP(tensor=attn_sinks.tensor, offset=attn_sinks.offset + 4 * g + a, ap=[[0, P], [2, 2]])
                pool.dma_start(sinkb[:, 4 * g + 2 * a:4 * g + 2 * a + 2], src, allow_slow_non_contiguous=True).then_inc(small_in, 16)
        pool.dma_start(farb[:], bcast(rel_bias_table[N_BUCKETS - 1, H_A:H_A + H_B], H_B)).then_inc(small_in, 16)
        pool.dma_start(subg[:], diff_subln_g[0].rearrange("(p a) -> p a", a=1)).then_inc(small_in, 16)
        pool.dma_start(lp[:].rearrange("p a b -> p (a b)"),
                       bcast(diff_lambda[0].rearrange("a b -> (a b)"), 4 * DH)).then_inc(small_in, 16)
        pool.wait_ge(pool_set, 1)
        pool.dma_start(acc[0:1, :, :].rearrange("p a b -> p (a b)"), b_ada).then_inc(bada_in, 16)

        def power(dst, src, done, n):
            pool.wait_ge(done, n)
            nc.gpsimd.tensor_tensor(dst, src, nhalf[:, 0:src.shape[1]], ALU.pow).then_inc(done, 1)

        pool.wait_ge(one_set, 2)
        power(rs[:, 2, :], rs[:, 1, :], xrs_step, 1)
        pool.wait_ge(mod_ps, 2)
        pool.dma_start(grow1[:], bcast(g_mix_post[0], D)).then_inc(grow_in, 16)
        pool.dma_start(grow2[:], bcast(g_ffn_pre[0], D)).then_inc(grow_in, 16)
        pool.wait_ge(hx_ready, TC)
        pool.dma_start(oh[:], oh_c).then_inc(oh_in, 16)
        pool.wait_ge(rv_ready, 2)
        pool.dma_start(bias_d[0:H_A, :], rv[:, 0, :]).then_inc(biasv_out, 16)
        pool.dma_start(bias_d[H_A:H_A + H_B, :], rv[0:H_B, 1, :]).then_inc(biasv_out, 16)
        pool.wait_ge(biasv_out, 32)
        pool.dma_start(wide_d, bass.AP(tensor=bias_d.tensor, offset=bias_d.offset,
                                       ap=[[REL, H_A + H_B], [0, P], [1, REL]])).then_inc(wide_out, 16)
        pool.wait_ge(wide_out, 16)

        def shifted(head, step, n):
            return bass.AP(tensor=wide_d.tensor, offset=wide_d.offset + head * P * REL + P - 1,
                           ap=[[REL - 1, P], [step * P * REL, n], [1, 2 * P]])

        for g in range(KV_A):
            for a in range(2):
                pool.dma_start(toep[:, 4 * g + 2 * a:4 * g + 2 * a + 2, :],
                               shifted(4 * g + a, 2, 2)).then_inc(toep_in, 16)
        pool.dma_start(toep[:, H_A:H_A + H_B, :], shifted(H_A, 1, H_B)).then_inc(toep_in, 16)
        pool.wait_ge(acc_done, 5 + 4 * N_W)
        pool.dma_start(grow3[:], bcast(g_ffn_post[0], D)).then_inc(grow_in, 16)
        for b in range(3):
            pool.dma_start(ball[32 * b:32 * b + 32, 0:2 * D], b_gate_up[0]).then_inc(ball_in, 16)
            pool.dma_start(ball[32 * b:32 * b + 32, 2 * D:3 * D], b_down[0]).then_inc(ball_in, 16)
        attention_pool(pool, power)
        merge_pool(pool, power)
        experts_pool(pool)
        final_pool(pool, power)


_INS = ['x', 'c', 'rel_bias_table', 'w_ada', 'b_ada', 'g_mix_pre', 'g_mix_post', 'g_ffn_pre', 'g_ffn_post', 'w_in',
        'w_out', 'attn_sinks', 'diff_lambda', 'diff_subln_g', 'w_router', 'b_router', 'w_gate_up', 'b_gate_up',
        'w_down', 'b_down']


def kernel(**inputs):
    import numpy as _np
    import concourse.bacc as _bacc
    from concourse import mybir as _mybir
    from concourse.bass_utils import run_bass_kernel_spmd as _run

    nc = _bacc.Bacc("TRN2", target_bir_lowering=False, num_devices=1)
    arrays, args = {}, []
    for name in _INS:
        a = _np.ascontiguousarray(inputs[name])
        arrays[f"in_{name}"] = a
        args.append(nc.dram_tensor(f"in_{name}", a.shape, _mybir.dt.from_np(a.dtype), kind="ExternalInput").ap())
    out = nc.dram_tensor("out_0", (1, T, D), F32, kind="ExternalOutput").ap()
    build(nc, *args, out)
    r = _run(nc, [arrays], core_ids=[0])
    return r.results[0]["out_0"]
```

```python
import math
from contextlib import ExitStack

import numpy as np

import concourse.bass as bass
from concourse import mybir

F32 = mybir.dt.float32
F32R = mybir.dt.float32r
BF16 = mybir.dt.bfloat16
I32 = mybir.dt.int32
U32 = mybir.dt.uint32
ALU = mybir.AluOpType
ACT = mybir.ActivationFunctionType
AX_X = mybir.AxisListType.X

P = 128
D = 1024
KC = D // P
T = 512
TC = T // P
H_A, KV_A, DH = 8, 2, 64
G_A = H_A // KV_A
H_B = 4
N_BUCKETS, MAX_EXACT, REL_MAX = 32, 16, 128
E = 32
TOPK = 4
FF = D
ALPHA, LIMIT = 1.702, 7.0
EPS, EPS_SUB = 1e-6, 1e-5
LAM_INIT = 0.8 - 0.6 * math.exp(0.0)
QK_SCALE = DH ** -0.5
MASKED = -1e30
PAD_ROW = 1 << 20
UN = 512
HK = KC // 2
NB = T // P
HALVES = 12
IN_FLIGHT, AHEAD = 4, 3
RAW, SPL = 4, 4
POOL_LOW = (7, 11)
DVE_LOW = tuple(v for v in range(HALVES) if v not in POOL_LOW)
REL = 2 * P + P

C_QA, C_KA, C_QB = 0, H_A * DH, (H_A + 2 * KV_A) * DH


def bucket(dist):
    n = np.maximum(dist, 0)
    nf = np.maximum(n, 1).astype(np.float32)
    large = MAX_EXACT + (np.log(nf / MAX_EXACT) / math.log(REL_MAX / MAX_EXACT)
                         * (N_BUCKETS - MAX_EXACT)).astype(np.int32)
    return np.where(n < MAX_EXACT, n, np.minimum(large, N_BUCKETS - 1))


def constants():
    ident = np.eye(P, dtype=np.float32)
    upper = np.triu(np.ones((P, P), np.float32), 1)
    dist = 255 - np.arange(REL)
    hot = (bucket(dist)[None, :] == np.arange(N_BUCKETS)[:, None])
    near = (dist >= 0) & (dist < P)
    causal = dist >= 0
    oh = np.zeros((N_BUCKETS + 1, 2, REL), np.float32)
    oh[:N_BUCKETS, 0], oh[N_BUCKETS, 0] = hot * near, ~near
    oh[:N_BUCKETS, 1], oh[N_BUCKETS, 1] = hot * causal, ~causal
    sel = np.tile(np.eye(E, E + 1, dtype=np.float32), (3, 1))
    pick = NB * np.triu(np.ones((E, E + 2), np.float32), 2) + np.eye(E, E + 2, 1, dtype=np.float32)
    iota_e = np.tile(np.arange(E, dtype=np.float32), (P, 1))
    tok = np.arange(TC)[None, :, None] * P + np.arange(P)[:, None, None]
    rows = (tok * TOPK + np.arange(TOPK)[None, None, :]).reshape(P, TC * TOPK).astype(np.int32)
    return ident, upper, oh.reshape(N_BUCKETS + 1, 2 * REL), sel, pick, iota_e, rows


def build(nc, x, c, rel_bias_table, w_ada, b_ada, g_mix_pre, g_mix_post, g_ffn_pre, g_ffn_post, w_in, w_out,
          attn_sinks, diff_lambda, diff_subln_g, w_router, b_router, w_gate_up, b_gate_up, w_down, b_down, out):
    ctx = ExitStack()
    with ctx:
        program(nc, ctx, x, c, rel_bias_table, w_ada, b_ada, g_mix_pre, g_mix_post, g_ffn_pre, g_ffn_post, w_in,
                w_out, attn_sinks, diff_lambda, diff_subln_g, w_router, b_router, w_gate_up, b_gate_up, w_down,
                b_down, out)


def program(nc, ctx, x, c, rel_bias_table, w_ada, b_ada, g_mix_pre, g_mix_post, g_ffn_pre, g_ffn_post, w_in, w_out,
            attn_sinks, diff_lambda, diff_subln_g, w_router, b_router, w_gate_up, b_gate_up, w_down, b_down, out):
    ident_c, upper_c, oh_c, sel_c, pick_c, iota_c, rows_c = [
        nc.inline_tensor(a, name=f"const_{n}").ap() for a, n in
        zip(constants(), ("ident", "upper", "buckets", "sel", "pick", "experts", "rows"))]

    def dram(name, shape, dt):
        return nc.dram_tensor(name, shape, dt, kind="Internal").ap()

    bias_d = dram("bias_vectors", (H_A + H_B, REL), F32)
    wide_d = dram("bias_vectors_repeated", (H_A + H_B, P, REL), F32)
    x1_d = dram("x_after_mixing", (T, D), F32)
    h2_d = dram("h_ffn", (T, D), F32)
    slot_d = dram("slot_rows", (T * E, 1), I32)
    y_d = dram("expert_rows", (T * TOPK, D), F32)

    base = 16512
    KB = 1024

    def at(name, shape, dt, off):
        return nc.alloc_sbuf_tensor_at(name, shape, dt, offset=base + off)

    raw = at("raw", [P, 4, HK, UN], F32, 0)
    whf = at("whf", [P, 2, HK, UN], F32R, 32 * KB)
    wlf = at("wlf", [P, 2, HK, UN], F32R, 48 * KB)
    hh = at("hh", [P, KC, T], F32R, 64 * KB)
    hl = at("hl", [P, KC, T], F32R, 80 * KB)
    s_sb = [at(f"s_sb{b}", [P, 1024], F32, off * KB) for b, off in enumerate((0, 4, 36, 40))]
    pt = at("pt", [P, 2, 1024], F32, 8 * KB)
    ota = at("ota", [P, H_A // 2, T], F32, 16 * KB)
    otb = at("otb", [P, H_B, T], F32, 24 * KB)
    on = at("on", [P, H_B, P], F32, 32 * KB)
    osq = at("osq", [P, P], F32, 34 * KB)
    ball = at("ball", [96, 3 * D], F32, 52 * KB)
    wo = at("wo", [P, KC, D], F32, 64 * KB)
    y1 = at("y1", [P, 2, D], F32, 0)
    y2 = at("y2", [P, 2, D], F32, 8 * KB)
    x1s = at("x1s", [P, 2, D], F32, 36 * KB)
    h2s = at("h2s", [P, 2, D], F32, 44 * KB)
    h2t = at("h2t", [P, KC, P], F32, 52 * KB)
    junk = at("junk", [P, D], F32, 56 * KB)
    wr = at("wr", [P, KC, E], F32, 60 * KB)
    oneh = at("oneh", [P, TC * TOPK, E], F32, 0)
    ohr = at("ohr", [P, TC * TOPK, E], F32, 2 * KB)
    rawm = at("rawm", [P, RAW, HK, UN], F32, 0)
    wh = at("wh", [P, SPL, HK, UN], F32R, 32 * KB)
    wl = at("wl", [P, SPL, HK, UN], F32R, 64 * KB)
    yt = at("yt", [P, 2, TOPK, D], F32, 0)
    x1e = at("x1e", [P, 2, D], F32, 32 * KB)
    yo = at("yo", [P, 2, D], F32, 40 * KB)
    fin = at("fin", [P, 2, D], F32, 48 * KB)
    junke = at("junke", [P, D], F32, 56 * KB)

    qk = at("qk", [P, 12, T], F32, 96 * KB)
    ka2 = at("ka2", [P, KV_A, T], F32, 120 * KB)
    nat = at("nat", [P, TC, 5 * UN], F32, 124 * KB)
    ht = at("ht", [P, KC, T], F32, 124 * KB)
    hx = at("hx", [P, 2, D], F32, 144 * KB)
    mrow = at("mrow", [1, 4, UN], F32, 96 * KB)
    bmods = at("bmods", [1, 4 * UN], F32, 106 * KB)
    gprec = at("gprec", [P, KC], F32, 104 * KB)
    gcol = at("gcol", [P, KC], F32, 104 * KB + 32)
    shcol = at("shcol", [P, KC], F32, 104 * KB + 64)
    xsq = at("xsq", [P, D], F32, 152 * KB)
    xs = at("xs", [P, TC, D], F32, 164 * KB)
    va = at("va", [P, TC, P], F32, 164 * KB)
    toep = at("toep", [P, H_A + H_B, 2 * P], F32, 166 * KB)
    rv = at("rv", [H_A, 2, REL], F32, 166 * KB)
    oh = at("oh", [N_BUCKETS + 1, 2 * REL], F32, 178 * KB)
    acc = at("acc", [P, 6, D], F32, 181 * KB)
    grow1 = at("grow1", [P, D], F32, 181 * KB)
    grow2 = at("grow2", [P, D], F32, 185 * KB)
    gpm = at("gpm", [P, D], F32, 189 * KB)
    shf = at("shf", [P, D], F32, 193 * KB)
    gf = at("gf", [P, D], F32, 197 * KB)
    gpf = at("gpf", [P, D], F32, 201 * KB)
    grow3 = at("grow3", [P, D], F32, 44 * KB)
    xh = at("xh", [P, NB, KC, P], F32R, 96 * KB)
    xl = at("xl", [P, NB, KC, P], F32R, 112 * KB)
    ah = at("ah", [P, NB, KC, P], F32R, 128 * KB)
    al = at("al", [P, NB, KC, P], F32R, 144 * KB)
    xg0 = at("xg0", [P, D], F32, 160 * KB)
    y0 = at("y0", [P, D], F32, 164 * KB)
    xy = [None] + [at(f"xy{b}", [P, D], F32, (164 + 4 * b) * KB) for b in range(1, NB)]
    gsu = at("gsu", [P, 2 + NB - 1, 3, 256], F32, 186 * KB)
    bparts = at("bparts", [96, 3 * D], BF16, 180 * KB)

    small_at = [205 * KB]

    def small(name, shape, dt):
        n = int(np.prod(shape[1:])) * (2 if dt == BF16 else 4)
        t = at(name, shape, dt, small_at[0])
        small_at[0] += -(-n // 32) * 32
        assert base + small_at[0] <= 229344
        return t

    ident = small("ident", [P, P], F32)
    gtab = small("gtab", [P, NB, E + 2], I32)
    stab = small("stab", [P, NB, E + 2], I32)
    topw = small("topw", [P, TC * TOPK], F32)
    sel = small("sel", [96, E + 1], BF16)
    icur = small("icur", [P, 2, NB], I32)
    nk = small("nk", [1, E + 2], I32)
    one = small("one", [P, 1], F32)
    nhalf = small("nhalf", [P, H_B], F32)
    cact = small("cact", [P, KC], F32)
    sinkb = small("sinkb", [P, H_A], F32)
    nsink = small("nsink", [P, H_A], F32)
    farb = small("farb", [P, H_B], F32)
    subg = small("subg", [P, 1], F32)
    subgs = small("subgs", [P, 1], F32)
    nlam0 = small("nlam0", [P, 1], F32)
    nlam = small("nlam", [P, 1], F32)
    tabx = small("tabx", [N_BUCKETS + 1, H_A + H_B], F32)
    rs = small("rs", [P, 3, TC], F32)
    rs1 = small("rs1", [P, 3, TC], F32)
    ccol = at("ccol", [P, KC], F32, 156 * KB)
    csig = at("csig", [P, KC], F32, 156 * KB + 32)
    lp = at("lp", [P, 4, DH], F32, 157 * KB)
    lprod = at("lprod", [P, 2, DH], F32, 158 * KB)
    lsum = at("lsum", [P, 2], F32, 159 * KB)
    lexp = at("lexp", [P, 2], F32, 159 * KB + 32)
    st = at("st", [P, IN_FLIGHT, 8, 4], F32, 35 * KB)
    NMX, MX, DSK, ESK, SUM, DEN, FAC = range(7)
    sn = at("sn", [P, 3, H_B], F32, 35 * KB + 512)

    r_at = [96 * KB]

    def route(name, shape, dt):
        n = int(np.prod(shape[1:])) * (2 if dt == BF16 else 4)
        t = at(name, shape, dt, r_at[0])
        r_at[0] += -(-n // 32) * 32
        assert r_at[0] <= 120 * KB
        return t

    lg = route("lg", [P, TC, E], F32)
    mv = route("mv", [P, TC, 8], F32)
    mi = route("mi", [P, TC, 8], U32)
    ef = route("ef", [P, TC, TOPK], F32)
    hot = route("hot", [P, TC, TOPK, E], F32)
    hotr = route("hotr", [P, TC, TOPK, E], F32)
    mask = route("mask", [P, TC, E], BF16)
    rsel = route("rsel", [P, TC * TOPK], F32)
    dest = route("dest", [P, TC * TOPK], I32)
    rows = route("rows", [P, TC * TOPK], I32)
    experts = route("experts", [P, E], F32)
    brow = route("brow", [P, E], F32)
    upperf = route("upperf", [P, P], F32)
    upper = route("upper", [P, P], BF16)
    onesb = route("onesb", [P, P], BF16)
    padt = route("padt", [P, P], I32)
    pick = route("pick", [E, E + 2], F32)
    over = route("over", [E, 4], F32)
    wexp = route("wexp", [P, TC, TOPK], F32)
    wsum = route("wsum", [P, 2, TC], F32)
    self_ = route("self", [96, E + 1], F32)
    begun = route("begun", [1, 2, E], F32)

    ps = ctx.enter_context(nc.psum_tensor("ps", [P, 8, UN], F32))

    def sem(name):
        return ctx.enter_context(nc.semaphore(name))

    bmods_in = sem("bmods_in")
    c_in, x_in, gpre_in, small_in, bada_in = map(sem, ("c_in", "x_in", "gpre_in", "small_in", "bada_in"))
    oh_in, biasv_out, wide_out, toep_in, wo_in, ball_in, grow_in = map(
        sem, ("oh_in", "biasv_out", "wide_out", "toep_in", "wo_in", "ball_in", "grow_in"))
    raw_in = [sem(f"raw_in{s}") for s in range(4)]
    pool_set, one_set, csig_ready, cact_ready, ada_step, raw_used = map(
        sem, ("pool_set", "one_set", "csig_ready", "cact_ready", "ada_step", "raw_used"))
    lam_step, lexp_ready = sem("lam_step"), sem("lexp_ready")
    mrow_ready, col_ps, col_ready, ht_copied = map(sem, ("mrow_ready", "col_ps", "col_ready", "ht_copied"))
    xss_ready, xrs_step, hx_ready, h_ready, ht_ps, hh_ready, hl_ready = map(
        sem, ("xss_ready", "xrs_step", "hx_ready", "h_ready", "ht_ps", "hh_ready", "hl_ready"))
    wh_ready, half0_used, acc_done, evac_done = map(sem, ("wh_ready", "half0_used", "acc_done", "evac_done"))
    rv_ps, rv_ready, tab_ready = sem("rv_ps"), sem("rv_ready"), sem("tab_ready")
    latemod_ps, latemod_ready, shf_ready = sem("latemod_ps"), sem("latemod_ready"), sem("shf_ready")
    s_ps, s_ready, mx_step, exp_ready, den_step, p_ready, t_ps, pt_ready, o_ps, o_ready = map(
        sem, ("s_ps", "s_ready", "mx_step", "exp_ready", "den_step", "p_ready", "t_ps", "pt_ready", "o_ps",
              "o_ready"))
    osq_ready, sn_ready, on_ready, ot_ps, ot_ready = map(
        sem, ("osq_ready", "sn_ready", "on_ready", "ot_ps", "ot_ready"))
    sig_gates, ya_ps, yb_ps, y1_ready, y2_ready, y_ready, yss_ready, yrs_step, yg_ready, x1_ready = map(
        sem, ("sig_gates", "ya_ps", "yb_ps", "y1_ready", "y2_ready", "y_ready", "yss_ready", "yrs_step", "yg_ready",
              "x1_ready"))
    x1ss_ready, x1rs_step, h2x_ready, h2_ready, h2t_ps, h2t_ready, lg_ps, lg_ready = map(
        sem, ("x1ss_ready", "x1rs_step", "h2x_ready", "h2_ready", "h2t_ps", "h2t_ready", "lg_ps", "lg_ready"))
    x1_out, h2_out = [sem("x1_out0"), sem("x1_out1")], [sem("h2_out0"), sem("h2_out1")]
    xr_in = [sem("xr_in0"), sem("xr_in1")]
    route_in, slot_init, route_step, rank_ps, dest_ready, slot_out, slot_in, tab_done = map(
        sem, ("route_in", "slot_init", "route_step", "rank_ps", "dest_ready", "slot_out", "slot_in", "tab_done"))
    over_ready, nk_ps, nk_ready, wdiff_ready, wexp_ready = map(
        sem, ("over_ready", "nk_ps", "nk_ready", "wdiff_ready", "wexp_ready"))
    y_out = [sem("y_out_0"), sem("y_out_more")]
    junk_step, top_step, dest_step, wsum_step = map(sem, ("junk_step", "top_step", "dest_step", "wsum_step"))
    bias_step = sem("bias_step")

    def halves(ap):
        return ap.rearrange("p (a b) -> p a b", a=2)

    def flat(ap):
        return ap.rearrange("p a b -> p (a b)")

    UNITS = [u for n in range(TC) for u in [("A", n, g) for g in range(KV_A)] + [("B", n, h) for h in range(H_B)]]
    N_T, N_N = 3, 5
    N_W = N_T + N_N
    N_BIAS = 7
    N_SMALL = 9

    def win_half(col, h, n=UN):
        return w_in[0, h * HK * P:(h + 1) * HK * P, col].rearrange("(k p) n -> p k n", p=P)

    def bcast(src, n):
        return bass.AP(tensor=src.tensor, offset=src.offset, ap=[[0, P], [1, n]])


    def total(count, i):
        return sum(count(u) for u in UNITS[:i + 1])

    def n_scores(u):
        return 2 if u[0] == "B" and u[1] >= 2 else 1

    def n_max(u):
        return 3 if u[0] == "A" else 2

    def n_exp(u):
        return 5 if u[0] == "A" else 2

    def n_den(u):
        return 2 if u[0] == "A" else 3

    def n_a(i):
        return sum(u[0] == "A" for u in UNITS[:i + 1])

    def keys(u):
        return (max(u[1] - 1, 0) if u[0] == "A" else 0), u[1] + 1

    def scores_ps(i):
        w = 2 * (i % 2)
        if UNITS[i][0] == "A":
            lo = P if UNITS[i][1] == 0 else 0
            return ps[:, w:w + 2, :].rearrange("p a (b k) -> p (a b) k", b=2)[:, :, lo:2 * P]
        return ps[:, w:w + 2, :]

    def scores_sb(i):
        if UNITS[i][0] == "A":
            lo = P if UNITS[i][1] == 0 else 0
            return s_sb[i % IN_FLIGHT][:].rearrange("p (a k) -> p a k", a=4)[:, :, lo:2 * P]
        return s_sb[i % IN_FLIGHT][:].rearrange("p (m k) -> p m k", m=2)[:, :, 0:keys(UNITS[i])[1] * P]

    def attention_pe(pe):
        def scores(i):
            kind, n, g = UNITS[i]
            w = 2 * (i % 2)
            if i >= 2:
                pe.wait_ge(s_ready, total(n_scores, i - 2))
            if kind == "A":
                k0, k1 = keys(UNITS[i])
                for place in range(4):
                    a, b = place // 2, place % 2
                    lo = (place % 2) * 2 * P + (P if n == 0 else 0)
                    ins = nc.tensor.matmul(ps[:, w + a, lo:lo + (k1 - k0) * P],
                                           qk[64 * a:64 * a + 64, 2 * g + b, n * P:(n + 1) * P],
                                           ka2[64 * a:64 * a + 64, g, k0 * P:k1 * P], start=True, stop=True)
            else:
                for m in range(2):
                    ins = nc.tensor.matmul(ps[:, w + m, 0:(n + 1) * P], qk[64 * m:64 * m + 64, 4 + g, n * P:(n + 1) * P],
                                           qk[64 * m:64 * m + 64, 8 + g, 0:(n + 1) * P], start=True, stop=True)
            ins.then_inc(s_ps, 1)

        def transposed(i):
            kind, n, g = UNITS[i]
            pe.wait_ge(p_ready, i + 1)
            if i == 0:
                pe.wait_ge(latemod_ready, 2)
            if i:
                pe.wait_ge(pt_ready, i)
            if kind == "A":
                for place in range(4):
                    for j in range(1 if n == 0 else 0, 2):
                        ins = nc.tensor.transpose(ps[:, 4 + place // 2, (place % 2 * 2 + j) * P:(place % 2 * 2 + j + 1) * P],
                                                  s_sb[i % IN_FLIGHT][:, (2 * place + j) * P:(2 * place + j + 1) * P], ident[:])
            else:
                for j in range(n + 1):
                    ins = nc.tensor.transpose(ps[:, 4, j * P:(j + 1) * P], s_sb[i % IN_FLIGHT][:, j * P:(j + 1) * P], ident[:])
            ins.then_inc(t_ps, 1)

        def values(i):
            kind, n, g = UNITS[i]
            pe.wait_ge(pt_ready, i + 1)
            if i == 0:
                pe.wait_ge(latemod_ready, 3)
            if kind == "A":
                if n_a(i) > 1:
                    pe.wait_ge(o_ready, n_a(i) - 1)
                if n >= 2 and g == 0:
                    pe.wait_ge(ot_ready, n - 1)
                js = range(1 if n == 0 else 0, 2)
                for place in range(4):
                    a, b = place // 2, place % 2
                    for j in js:
                        ins = nc.tensor.matmul(ps[64 * a:64 * a + 64, 6, b * P:(b + 1) * P],
                                               va[:, n - 1 + j, 64 * g:64 * g + 64],
                                               pt[:, i % 2, (2 * place + j) * P:(2 * place + j + 1) * P],
                                               start=(j == js[0]), stop=(j == 1))
            else:
                if n and g == 0:
                    pe.wait_ge(on_ready, n)
                for j in range(n + 1):
                    ins = nc.tensor.matmul(ps[:, 7, g * P:(g + 1) * P], pt[:, i % 2, j * P:(j + 1) * P],
                                           nat[:, j, g * P:(g + 1) * P], start=(j == 0), stop=(j == n))
            ins.then_inc(o_ps, 1)

        def outputs_transposed(n):
            pe.wait_ge(on_ready, n + 1)
            pe.wait_ge(o_ready, min(2 * n + 4, 2 * TC))
            for h in range(H_B):
                ins = nc.tensor.transpose(ps[:, 6, h * P:(h + 1) * P], on[:, h, :], ident[:])
            ins.then_inc(ot_ps, 1)

        for i in range(AHEAD):
            scores(i)
        for i in range(len(UNITS)):
            transposed(i)
            if i + AHEAD < len(UNITS):
                scores(i + AHEAD)
            values(i)
            if i >= 2 and UNITS[i - 2][0] == "B" and UNITS[i - 2][2] == H_B - 1:
                outputs_transposed(UNITS[i - 2][1])
        outputs_transposed(TC - 1)

    def attention_dve(dve):
        dve.wait_ge(toep_in, 16 * 5)

        def before(i):
            kind, n, g = UNITS[i]
            w = i % IN_FLIGHT
            if i >= IN_FLIGHT:
                dve.wait_ge(t_ps, i - IN_FLIGHT + 1)
            dve.wait_ge(s_ps, i + 1)
            src, dst = scores_ps(i), scores_sb(i)
            if kind == "A":
                lo = P if n == 0 else 0
                nc.vector.scalar_tensor_tensor(dst, src, QK_SCALE, toep[:, 4 * g:4 * g + 4, lo:2 * P], ALU.mult,
                                               ALU.add).then_inc(s_ready, 1)
                dve.wait_ge(s_ready, total(n_scores, i))
                nc.vector.tensor_reduce(st[:, w, MX, :], dst, AX_X, ALU.max).then_inc(mx_step, 1)
                dve.wait_ge(mx_step, total(n_max, i) - 2)
                nc.vector.scalar_tensor_tensor(st[:, w, NMX, :], st[:, w, MX, :], -1.0, nsink[:, 4 * g:4 * g + 4],
                                               ALU.mult, ALU.min).then_inc(mx_step, 1)
                dve.wait_ge(mx_step, total(n_max, i) - 1)
                nc.vector.tensor_tensor(st[:, w, DSK, :], st[:, w, NMX, :], sinkb[:, 4 * g:4 * g + 4],
                                        ALU.add).then_inc(mx_step, 1)
                return
            near = max(n - 1, 0) * P
            width = (n + 1) * P - near
            tile = toep[:, H_A + g:H_A + g + 1, 2 * P - width:2 * P].to_broadcast([P, 2, width])
            nc.vector.scalar_tensor_tensor(dst[:, :, near:near + width], src[:, :, near:near + width], QK_SCALE, tile,
                                           ALU.mult, ALU.add).then_inc(s_ready, 1)
            if near:
                nc.vector.tensor_scalar(dst[:, :, 0:near], src[:, :, 0:near], QK_SCALE, farb[:, g:g + 1], ALU.mult,
                                        ALU.add).then_inc(s_ready, 1)
            dve.wait_ge(s_ready, total(n_scores, i))
            nc.vector.tensor_reduce(st[:, w, MX, 0:2], dst, AX_X, ALU.max).then_inc(mx_step, 1)
            dve.wait_ge(mx_step, total(n_max, i) - 1)
            nc.vector.tensor_scalar(st[:, w, NMX, 0:2], st[:, w, MX, 0:2], -1.0, None, ALU.mult).then_inc(mx_step, 1)

        def after(i):
            kind, n, g = UNITS[i]
            w = i % IN_FLIGHT
            dst = scores_sb(i)
            width = dst.shape[2]
            dve.wait_ge(exp_ready, total(n_exp, i))
            if kind == "A":
                nc.vector.tensor_tensor(st[:, w, DEN, :], st[:, w, SUM, :], st[:, w, ESK, :], ALU.add).then_inc(den_step, 1)
                dve.wait_ge(den_step, total(n_den, i) - 1)
                nc.vector.reciprocal(st[:, w, FAC, :], st[:, w, DEN, :]).then_inc(den_step, 1)
                dve.wait_ge(den_step, total(n_den, i))
                nc.vector.tensor_tensor(dst, dst, st[:, w, FAC, :].unsqueeze(2).to_broadcast([P, 4, width]),
                                        ALU.mult).then_inc(p_ready, 1)
                return
            nc.vector.reciprocal(st[:, w, FAC, 0:2], st[:, w, SUM, 0:2]).then_inc(den_step, 1)
            dve.wait_ge(den_step, total(n_den, i) - 2)
            nc.vector.tensor_tensor(st[:, w, DEN, 0:1], st[:, w, FAC, 1:2], nlam[:], ALU.mult).then_inc(den_step, 1)
            nc.vector.tensor_scalar(dst[:, 0, :], dst[:, 0, :], st[:, w, FAC, 0:1], None, ALU.mult).then_inc(den_step, 1)
            dve.wait_ge(den_step, total(n_den, i))
            nc.vector.scalar_tensor_tensor(dst[:, 0, :], dst[:, 1, :], st[:, w, DEN, 0:1], dst[:, 0, :], ALU.mult,
                                           ALU.add).then_inc(p_ready, 1)

        def bias_parts(n):
            if n == 0:
                dve.wait_ge(ball_in, 16 * 6)
                dve.wait_ge(latemod_ready, 3)
                nc.vector.tensor_copy(bparts[:], ball[:]).then_inc(bias_step, 1)
                return
            cut, lo = ((False, 1), (False, 2), (True, 1), (True, 2), (False, 2), (True, 2))[n - 1]
            rows = slice(32 * lo, 32 * lo + 32)
            dve.wait_ge(bias_step, n)
            if cut:
                nc.vector.tensor_copy(bparts[rows, :], ball[rows, :]).then_inc(bias_step, 1)
            else:
                nc.vector.tensor_tensor(ball[rows, :], ball[rows, :], bparts[rows, :], ALU.subtract).then_inc(bias_step, 1)

        def sub_norm(n):
            dve.wait_ge(osq_ready, H_B * (n + 1))
            nc.vector.tensor_scalar(sn[:, 1, :], sn[:, 0, :], 1.0 / (2 * DH), EPS_SUB, ALU.mult,
                                    ALU.add).then_inc(sn_ready, 1)
            dve.wait_ge(sn_ready, 2 * n + 2)
            if n:
                dve.wait_ge(ot_ps, n)
            nc.vector.tensor_tensor(on[:], ps[:, 7, :].rearrange("p (h d) -> p h d", h=H_B),
                                    sn[:, 2, :].unsqueeze(2).to_broadcast([P, H_B, P]), ALU.mult).then_inc(on_ready, 1)

        for i in range(AHEAD):
            before(i)
        dve.wait_ge(grow_in, 48)
        dve.wait_ge(latemod_ps, 4)
        nc.vector.tensor_tensor(halves(gpf[:]), ps[:, 6:8, :], halves(grow3[:]), ALU.mult).then_inc(latemod_ready, 1)
        after(0)
        for i in range(len(UNITS)):
            if i + 1 < len(UNITS):
                after(i + 1)
            if i + AHEAD < len(UNITS):
                before(i + AHEAD)
            if i and UNITS[i - 1][0] == "B" and UNITS[i - 1][2] == H_B - 1:
                sub_norm(UNITS[i - 1][1])
            if 8 <= i < 8 + N_BIAS:
                bias_parts(i - 8)
        sub_norm(TC - 1)

    def attention_act(act):
        def exps(i):
            kind, n, g = UNITS[i]
            w = i % IN_FLIGHT
            dst = scores_sb(i)
            act.wait_ge(mx_step, total(n_max, i))
            for m in range(dst.shape[1]):
                nc.scalar.activation(dst[:, m, :], dst[:, m, :], ACT.Exp, bias=st[:, w, NMX, m:m + 1],
                                     accum_out=st[:, w, SUM, m:m + 1]).then_inc(exp_ready, 1)
            if kind == "A":
                nc.scalar.activation(st[:, w, ESK, :], st[:, w, DSK, :], ACT.Exp).then_inc(exp_ready, 1)

        def copies(i):
            kind, n, g = UNITS[i]
            act.wait_ge(t_ps, i + 1)
            if i >= 2:
                act.wait_ge(o_ps, i - 1)
            if kind == "A":
                lo = P if n == 0 else 0
                src = ps[:, 4:6, :].rearrange("p a (b k) -> p (a b) k", b=2)[:, :, lo:2 * P]
                dst = pt[:, i % 2, :].rearrange("p (a k) -> p a k", a=4)[:, :, lo:2 * P]
            else:
                src, dst = ps[:, 4, 0:(n + 1) * P], pt[:, i % 2, 0:(n + 1) * P]
            nc.scalar.activation(dst, src, ACT.Copy).then_inc(pt_ready, 1)
            act.wait_ge(o_ps, i + 1)
            if kind == "A":
                nc.scalar.activation(ota[:, 2 * g:2 * g + 2, n * P:(n + 1) * P],
                                     ps[:, 6, 0:2 * P].rearrange("p (a q) -> p a q", a=2), ACT.Copy).then_inc(o_ready, 1)
            elif g == H_B - 1:
                for h in range(H_B):
                    if n or h:
                        act.wait_ge(osq_ready, H_B * n + h)
                    nc.scalar.activation(osq[:], ps[:, 7, h * P:(h + 1) * P], ACT.Square,
                                         accum_out=sn[:, 0, h:h + 1]).then_inc(osq_ready, 1)

        def outputs_transposed(n):
            act.wait_ge(ot_ps, n + 1)
            nc.scalar.activation(otb[:, :, n * P:(n + 1) * P], ps[:, 6, :].rearrange("p (h q) -> p h q", h=H_B),
                                 ACT.Identity, scale=subgs[:, 0:1]).then_inc(ot_ready, 1)

        for i in range(AHEAD):
            exps(i)
        for i in range(len(UNITS)):
            copies(i)
            if i + AHEAD < len(UNITS):
                exps(i + AHEAD)
            if i >= 2 and UNITS[i - 2][0] == "B" and UNITS[i - 2][2] == H_B - 1:
                outputs_transposed(UNITS[i - 2][1])
        outputs_transposed(TC - 1)

    def attention_pool(pool, power):
        for n in range(TC):
            power(sn[:, 2, :], sn[:, 1, :], sn_ready, 2 * n + 1)

    def merge_pe(pe):
        pe.wait_ge(wo_in, 32)

        def branches(t):
            pe.wait_ge(o_ready, 2 * (t + 1))
            pe.wait_ge(ot_ready, t + 1)
            if t == 0:
                pe.wait_ge(p_ready, len(UNITS))
            for b, (src, free, done) in enumerate(((ota, y1_ready, ya_ps), (otb, y2_ready, yb_ps))):
                if t:
                    pe.wait_ge(free, t)
                for half in range(2):
                    for k in range(4):
                        ins = nc.tensor.matmul(ps[:, 2 * b + half, :], src[:, k, t * P:(t + 1) * P],
                                               wo[:, 4 * b + k, half * UN:(half + 1) * UN], start=(k == 0), stop=(k == 3))
                ins.then_inc(done, 1)

        def router(t):
            pe.wait_ge(h2_ready, t + 1)
            if t == 0:
                pe.wait_ge(pt_ready, len(UNITS))
                pe.wait_ge(ot_ready, TC)
                pe.wait_ge(route_in, 16 * N_ROUTE)
            else:
                pe.wait_ge(h2t_ready, t)
            for k in range(KC):
                ins = nc.tensor.transpose(ps[:, 4 + k // 4, (k % 4) * P:(k % 4 + 1) * P],
                                          h2s[:, t % 2, k * P:(k + 1) * P], ident[:])
            ins.then_inc(h2t_ps, 1)
            pe.wait_ge(h2t_ready, t + 1)
            if t:
                pe.wait_ge(lg_ready, t)
            for k in range(KC):
                ins = nc.tensor.matmul(ps[:, 6, 0:E], h2t[:, k, :], wr[:, k, :], start=(k == 0), stop=(k == KC - 1))
            ins.then_inc(lg_ps, 1)

        branches(0)
        for t in range(TC):
            if t + 1 < TC:
                branches(t + 1)
            router(t)
        pe.wait_ge(route_step, MASKS_DONE)
        for t in range(TC):
            for s in range(t + 1):
                ins = nc.tensor.matmul(ps[:, 6, t * E:(t + 1) * E], upper[:] if s == t else onesb[:],
                                       mask[:, s, :], start=(s == 0), stop=(s == t))
        ins.then_inc(rank_ps, 1)
        for t in range(TC):
            ins = nc.tensor.matmul(ps[0:E, 7, 0:1], mask[:, t, :], onesb[:, 0:1], start=(t == 0), stop=(t == TC - 1))
        ins.then_inc(rank_ps, 1)
        pe.wait_ge(over_ready, 4)
        nc.tensor.matmul(ps[0:1, 5, 0:E + 2], over[:, 3:4], pick[:], start=True, stop=True).then_inc(nk_ps, 1)

    MASKS_DONE = 6

    def merge_act(act):
        for t in range(TC):
            nc.scalar.activation(nat[:, t, UN:], nat[:, t, UN:], ACT.Sigmoid).then_inc(sig_gates, 1)
        n_junk = [0]

        def square(src, dst):
            if n_junk[0]:
                act.wait_ge(junk_step, n_junk[0])
            nc.scalar.activation(junk[:], src, ACT.Square, accum_out=dst).then_inc(junk_step, 1)
            n_junk[0] += 1

        for t in range(TC):
            act.wait_ge(y_ready, t + 1)
            square(y1[:, t % 2, :], rs[:, 0, t:t + 1])
            act.wait_ge(x1_ready, t + 1)
            square(x1s[:, t % 2, :], rs1[:, 0, t:t + 1])
            act.wait_ge(h2t_ps, t + 1)
            if t:
                act.wait_ge(lg_ps, t)
            nc.scalar.activation(flat(h2t[:]), flat(ps[:, 4:6, :]), ACT.Copy).then_inc(h2t_ready, 1)
        act.wait_ge(wdiff_ready, 1)
        nc.scalar.activation(wexp[:], wexp[:], ACT.Exp).then_inc(wexp_ready, 1)

    def merge_dve(dve):
        for t in range(TC):
            w = t % 2
            dve.wait_ge(sig_gates, t + 1)
            dve.wait_ge(ya_ps, t + 1)
            nc.vector.tensor_tensor(y1[:, w, :].rearrange("p (a b) -> p a b", a=2), ps[:, 0:2, :],
                                    nat[:, t, UN:UN + D].rearrange("p (a b) -> p a b", a=2), ALU.mult).then_inc(y1_ready, 1)
            dve.wait_ge(yb_ps, t + 1)
            nc.vector.tensor_tensor(y2[:, w, :].rearrange("p (a b) -> p a b", a=2), ps[:, 2:4, :],
                                    nat[:, t, UN + D:].rearrange("p (a b) -> p a b", a=2), ALU.mult).then_inc(y2_ready, 1)
            dve.wait_ge(y1_ready, t + 1)
            dve.wait_ge(y2_ready, t + 1)
            nc.vector.tensor_tensor(y1[:, w, :], y1[:, w, :], y2[:, w, :], ALU.add).then_inc(y_ready, 1)
            dve.wait_ge(junk_step, 2 * t + 1)
            nc.vector.tensor_scalar(rs[:, 1, t:t + 1], rs[:, 0, t:t + 1], 1.0 / D, EPS, ALU.mult,
                                    ALU.add).then_inc(yrs_step, 1)
            dve.wait_ge(yrs_step, 2 * t + 2)
            dve.wait_ge(y_ready, t + 1)
            nc.vector.scalar_tensor_tensor(y2[:, w, :], y1[:, w, :], rs[:, 2, t:t + 1], gpm[:], ALU.mult,
                                           ALU.mult).then_inc(yg_ready, 1)
            dve.wait_ge(yg_ready, t + 1)
            dve.wait_ge(xr_in[w], 16 * (t // 2 + 1))
            nc.vector.tensor_tensor(x1s[:, w, :], x1s[:, w, :], y2[:, w, :], ALU.add).then_inc(x1_ready, 1)
            dve.wait_ge(junk_step, 2 * t + 2)
            nc.vector.tensor_scalar(rs1[:, 1, t:t + 1], rs1[:, 0, t:t + 1], 1.0 / D, EPS, ALU.mult,
                                    ALU.add).then_inc(x1rs_step, 1)
            dve.wait_ge(x1rs_step, 2 * t + 2)
            dve.wait_ge(x1_ready, t + 1)
            nc.vector.scalar_tensor_tensor(y1[:, w, :], x1s[:, w, :], rs1[:, 2, t:t + 1], gf[:], ALU.mult,
                                           ALU.mult).then_inc(h2x_ready, 1)
            dve.wait_ge(h2x_ready, t + 1)
            if t >= 2:
                dve.wait_ge(h2_out[w], 16 * (t // 2))
                dve.wait_ge(h2t_ps, t - 1)
            nc.vector.tensor_tensor(h2s[:, w, :], y1[:, w, :], shf[:], ALU.add).then_inc(h2_ready, 1)
            dve.wait_ge(lg_ps, t + 1)
            nc.vector.tensor_tensor(lg[:, t, :], ps[:, 6, 0:E], brow[:], ALU.add).then_inc(lg_ready, 1)
        dve.wait_ge(lg_ready, TC)
        for t in range(TC):
            nc.vector.max(mv[:, t, :], lg[:, t, :]).then_inc(top_step, 1)
        dve.wait_ge(top_step, TC)
        for t in range(TC):
            nc.vector.max_index(mi[:, t, :], mv[:, t, :], lg[:, t, :]).then_inc(top_step, 1)
        dve.wait_ge(top_step, 2 * TC)
        nc.vector.tensor_copy(ef[:], mi[:, :, 0:TOPK]).then_inc(route_step, 1)
        nc.vector.tensor_copy(upper[:], upperf[:]).then_inc(route_step, 1)
        nc.vector.memset(onesb[:], 1.0).then_inc(route_step, 1)
        nc.vector.tensor_copy(sel[:], self_[:]).then_inc(route_step, 1)
        dve.wait_ge(route_step, 4)
        hotf = hot[:].rearrange("p t j e -> p (t j) e")
        hotrf = hotr[:].rearrange("p t j e -> p (t j) e")
        eff = ef[:].rearrange("p t j -> p (t j)")
        nc.vector.tensor_tensor(hotf, experts[:].unsqueeze(1).to_broadcast([P, TC * TOPK, E]),
                                eff.unsqueeze(2).to_broadcast([P, TC * TOPK, E]), ALU.is_equal).then_inc(route_step, 1)
        dve.wait_ge(route_step, 5)
        with nc.allow_low_precision(reason="sums of 0 and 1 that are 0 or 1"):
            nc.vector.tensor_reduce(mask[:], hot[:].rearrange("p t j e -> p t e j"), AX_X,
                                    ALU.add).then_inc(route_step, 1)
        nc.vector.tensor_tensor(wexp[:], mv[:, :, 0:TOPK], mv[:, :, 0:1].to_broadcast([P, TC, TOPK]),
                                ALU.subtract).then_inc(wdiff_ready, 1)
        dve.wait_ge(rank_ps, 1)
        nc.vector.tensor_tensor(hotr[:], hot[:],
                                ps[:, 6, 0:TC * E].rearrange("p (t e) -> p t e", t=TC).unsqueeze(2).to_broadcast(
                                    [P, TC, TOPK, E]), ALU.mult).then_inc(dest_step, 1)
        dve.wait_ge(dest_step, 1)
        nc.vector.tensor_reduce(rsel[:], hotrf, AX_X, ALU.add).then_inc(dest_step, 1)
        dve.wait_ge(dest_step, 2)
        nc.vector.scalar_tensor_tensor(dest[:], rsel[:], float(E), eff, ALU.mult, ALU.add).then_inc(dest_ready, 1)
        dve.wait_ge(rank_ps, 2)
        for b in range(NB - 1):
            nc.vector.tensor_scalar(over[:, b:b + 1], ps[0:E, 7, 0:1], (b + 1) * P + 0.5, None,
                                    ALU.is_gt).then_inc(over_ready, 1)
        dve.wait_ge(over_ready, NB - 1)
        nc.vector.tensor_reduce(over[:, 3:4], over[:, 0:3], AX_X, ALU.add).then_inc(over_ready, 1)
        dve.wait_ge(nk_ps, 1)
        nc.vector.tensor_copy(nk[:], ps[0:1, 5, 0:E + 2]).then_inc(nk_ready, 1)
        dve.wait_ge(wexp_ready, 1)
        nc.vector.tensor_reduce(wsum[:, 0, :], wexp[:], AX_X, ALU.add).then_inc(wsum_step, 1)
        dve.wait_ge(wsum_step, 1)
        nc.vector.reciprocal(wsum[:, 1, :], wsum[:, 0, :]).then_inc(wsum_step, 1)
        dve.wait_ge(wsum_step, 2)
        nc.vector.tensor_tensor(topw[:].rearrange("p (t j) -> p t j", t=TC), wexp[:],
                                wsum[:, 1, :].unsqueeze(2).to_broadcast([P, TC, TOPK]), ALU.mult).then_inc(wsum_step, 1)
        dve.wait_ge(slot_in, 16)
        nc.vector.tensor_scalar(gtab[:], stab[:], 2, None, ALU.arith_shift_right).then_inc(tab_done, 1)

    N_ROUTE = 7

    def merge_pool(pool, power):
        pool.wait_ge(pt_ready, len(UNITS))
        pool.dma_start(wr[:], w_router[0].rearrange("(k p) e -> p k e", p=P)).then_inc(route_in, 16)
        pool.dma_start(brow[:], bcast(b_router[0], E)).then_inc(route_in, 16)
        pool.dma_start(upperf[:], upper_c).then_inc(route_in, 16)
        pool.dma_start(experts[:], iota_c).then_inc(route_in, 16)
        pool.dma_start(rows[:], rows_c).then_inc(route_in, 16)
        pool.dma_start(pick[:], pick_c).then_inc(route_in, 16)
        pool.dma_start(self_[:], sel_c).then_inc(route_in, 16)
        for m in range(2):
            pool.dma_start(begun[0:1, m, :], iota_c[0:1, :]).then_inc(y_out[m], 16)
        nc.gpsimd.memset(padt[:], PAD_ROW).then_inc(pool_set, 1)
        nc.gpsimd.memset(stab[:], PAD_ROW).then_inc(pool_set, 1)
        pool.wait_ge(pool_set, 3)
        pool.dma_start(slot_d.rearrange("(p a) b -> p (a b)", p=P), padt[:]).then_inc(slot_init, 16)
        for t in range(TC):
            power(rs[:, 2, t:t + 1], rs[:, 1, t:t + 1], yrs_step, 2 * t + 1)
            power(rs1[:, 2, t:t + 1], rs1[:, 1, t:t + 1], x1rs_step, 2 * t + 1)
        pool.wait_ge(dest_ready, 1)
        pool.wait_ge(slot_init, 16)
        for i in range(TC * TOPK):
            pool.indirect_dma_start(out=slot_d, out_offset=bass.IndirectOffsetOnAxis(ap=dest[:, i:i + 1], axis=0),
                                    in_=rows[:, i:i + 1], in_offset=None).then_inc(slot_out, 16)
        pool.wait_ge(slot_out, 16 * TC * TOPK)
        pool.dma_start(stab[:, :, 1:E + 1], slot_d.rearrange("(b p e) a -> p b (e a)", b=NB, p=P)).then_inc(slot_in, 16)

    def merge_sync(sp):
        sp.wait_ge(t_ps, len(UNITS))
        for t in range(2):
            sp.dma_start(x1s[:, t, :], x[0, t * P:(t + 1) * P, :]).then_inc(xr_in[t], 16)
        for t in range(TC):
            w = t % 2
            sp.wait_ge(x1_ready, t + 1)
            sp.dma_start(x1_d[t * P:(t + 1) * P, :], x1s[:, w, :]).then_inc(x1_out[w], 16)
            sp.wait_ge(h2_ready, t + 1)
            sp.dma_start(h2_d[t * P:(t + 1) * P, :], h2s[:, w, :]).then_inc(h2_out[w], 16)
            if t < 2:
                sp.wait_ge(x1_out[w], 16)
                sp.dma_start(x1s[:, w, :], x[0, (t + 2) * P:(t + 3) * P, :]).then_inc(xr_in[w], 16)

    half_used, acc_more, wh_done, wl_done, wl_pool_done = map(
        sem, ("half_used", "acc_more", "wh_done", "wl_done", "wl_pool_done"))
    rawm_in = [sem(f"rawm_in{s}") for s in range(RAW)]
    pair = lambda name: (sem(name + "_0"), sem(name + "_more"))
    xg_in, xt_done, xh_done, xl_done, gcur, scur = map(pair, ("xg_in", "xt_done", "xh_done", "xl_done", "gcur", "scur"))
    g_ready, acc_free, up_ready, s_done, act_ready, at_done, ah_done, al_done, y_copied = map(
        pair, ("g_ready", "acc_free", "up_ready", "s_done", "act_ready", "at_done", "ah_done", "al_done", "y_copied"))
    y_half_copied = [sem("y_half_copied0"), y_copied[0]]
    pool_passed = sem("pool_passed")
    START = 1
    from_one = [s for p in (xt_done, xh_done, xl_done, gcur, scur, g_ready, acc_free, up_ready, s_done, act_ready,
                            at_done, ah_done, al_done, y_copied, (y_half_copied[0], acc_more)) for s in p]
    T_GU, U_ALL = 4, 6

    class Expert:

        def __init__(self, eng, e):
            self.eng, self.e = eng, e
            both = eng.value_load(nk[0:1, bass.ds(e + 1, 1)], min_val=0, max_val=NB * (T * TOPK // P) + NB - 1)
            self.before = eng.snap(both // NB)
            self.more = eng.snap(both % NB)

        def count(self, steps, step, b):
            if b == 0:
                return self.e * steps + step + 1 + START
            return self.before * steps + self.more * step + b + START

        def all_more(self, steps, step):
            return self.before * steps + self.more * (step + 1) + START

        def earlier(self, steps, b):
            return (self.before if b else self.e) * steps + START

        def stored(self, b):
            return ((self.before if b else self.e) + START) * 16

        def blocks(self, work):
            self.further(work)
            work(0)

        def further(self, work):
            with self.eng.If(self.more >= 1):
                work(1)
                for b in range(2, NB):
                    with self.eng.If(self.more >= b):
                        work(b)

    def weights(e, v):
        rows = slice(v % 2 * HK * P, (v % 2 + 1) * HK * P)
        if v < 2 * T_GU:
            t = v // 2
            return [w_gate_up[0, bass.ds(e, 1), rows, up * FF + 256 * t:up * FF + 256 * (t + 1)].rearrange(
                "a (k p) n -> p (a k) n", p=P) for up in range(2)]
        t = v // 2 - T_GU
        return [w_down[0, bass.ds(e, 1), rows, UN * t:UN * (t + 1)].rearrange("a (k p) n -> p (a k) n", p=P)]

    def loaded(e, v):
        gain = lambda halves: sum(32 if x < 2 * T_GU else 16 for x in halves)
        return e * gain(range(v % RAW, HALVES, RAW)) + gain(range(v % RAW, v + 1, RAW))

    def wait_low(eng, e, v):
        if v in POOL_LOW:
            eng.wait_ge(wl_pool_done, e * len(POOL_LOW) + (POOL_LOW.index(v) + 1))
        else:
            eng.wait_ge(wl_done, e * len(DVE_LOW) + (DVE_LOW.index(v) + 1))

    def experts_sync(sp):
        sp.wait_ge(h2t_ps, TC)
        for w in range(2):
            sp.wait_ge(x1_out[w], 32)
            sp.wait_ge(h2_out[w], 32)

        def load(e, v):
            for n, src in enumerate(weights(e, v)):
                dst = rawm[:, v % RAW, :, :] if v >= 2 * T_GU else rawm[:, v % RAW, :, 256 * n:256 * (n + 1)]
                sp.dma_start(dst, src).then_inc(rawm_in[v % RAW], 16)

        for v in range(RAW):
            load(0, v)

        def rest(e, ahead):
            for v in range(RAW, HALVES + (RAW if ahead else 0)):
                wait_low(sp, e, v - RAW)
                load(e + v // HALVES, v % HALVES)

        with sp.Fori(0, E - 1) as e:
            rest(e, True)
        rest(E - 1, False)

    def experts_pe(pe):
        pe.wait_ge(nk_ready, 1)

        def tokens_transposed(x):
            def work(b):
                m = min(b, 1)
                if b:
                    pe.wait_ge(xg_in[1], (x.before + x.more) * 16)
                    pe.wait_ge(xl_done[1], x.count(1, 0, b) - 1)
                else:
                    pe.wait_ge(xg_in[0], (x.e + 1) * 16)
                    pe.wait_ge(xl_done[1], x.all_more(1, 0))
                pe.wait_ge(xl_done[0], x.earlier(1, 0))
                src = xy[b] if b else xg0
                for k in range(KC):
                    ins = nc.tensor.transpose(ps[:, 5 + k // 4, (k % 4) * P:(k % 4 + 1) * P], src[:, k * P:(k + 1) * P],
                                              ident[:])
                ins.then_inc(xt_done[m], 1)
            x.blocks(work)

        def act_transposed(x, t):
            def work(b):
                m = min(b, 1)
                pe.wait_ge(act_ready[m], x.count(T_GU, t, b))
                pe.wait_ge(al_done[0], x.e * T_GU + t + START)
                pe.wait_ge(al_done[1], x.count(T_GU, t, b) - 1 if b else x.all_more(T_GU, t))
                for j in range(2):
                    ins = nc.tensor.transpose(ps[:, 7, j * P:(j + 1) * P],
                                              gsu[:, 1 + b if b else t % 2, 2, j * P:(j + 1) * P], ident[:])
                ins.then_inc(at_done[m], 1)
            x.blocks(work)

        def half(x, v):
            u, h = v // 2, v % 2
            wait_low(pe, x.e, v)

            def work(b):
                bank = 1 + b if b else u % 2
                dst = ps[:, bank, :]
                if v == 0:
                    pe.wait_ge(xl_done[min(b, 1)], x.all_more(1, 0) if b else x.count(1, 0, 0))
                if v == 8 or v == 9:
                    tiles = 2 if v == 8 else 4
                    pe.wait_ge(al_done[min(b, 1)], x.all_more(T_GU, tiles - 1) if b else x.count(T_GU, tiles - 1, 0))
                if h == 0:
                    if b == 0:
                        if u <= 1:
                            pe.wait_ge(y_half_copied[u], x.earlier(1, 0))
                        else:
                            pe.wait_ge(acc_free[0], x.count(T_GU, u - 2, 0))
                    elif u == 0:
                        pe.wait_ge(y_copied[1], x.earlier(2, 1))
                    elif u <= T_GU:
                        pe.wait_ge(acc_free[1], x.count(T_GU, u - 1, b))
                    else:
                        pe.wait_ge(y_copied[1], x.count(2, 0, b))
                    if u < T_GU:
                        bias = bparts[:, 0:2 * D].rearrange("p (a n) -> p a n", a=2)[:, :, 256 * u:256 * (u + 1)]
                    else:
                        bias = bparts[:, 2 * D + UN * (u - T_GU):2 * D + UN * (u - T_GU + 1)]
                    nc.tensor.matmul(dst, sel[:, bass.ds(x.e, 1)].to_broadcast([96, P]), bias, start=True, stop=False)
                a_h, a_l = (xh, xl) if u < T_GU else (ah, al)
                for k in range(HK):
                    kk = HK * h + k
                    nc.tensor.matmul(dst, a_h[:, b, kk, :], wh[:, v % SPL, k, :], start=False, stop=False)
                    nc.tensor.matmul(dst, a_h[:, b, kk, :], wl[:, v % SPL, k, :], start=False, stop=False)
                    ins = nc.tensor.matmul(dst, a_l[:, b, kk, :], wh[:, v % SPL, k, :], start=False, stop=kk == KC - 1)
                if b == 0:
                    ins.then_inc(half_used, 1)
                elif h:
                    ins.then_inc(acc_more, 1)
            x.blocks(work)

        tokens_transposed(Expert(pe, 0))
        pe.wait_ge(nk_ready, 1)
        with pe.Fori(0, E) as e:
            x = Expert(pe, e)
            for v in range(9):
                half(x, v)
                if v in (3, 5, 7):
                    act_transposed(x, (v - 3) // 2)
            act_transposed(x, 3)
            tokens_transposed(Expert(pe, e + 1))
            for v in range(9, HALVES):
                half(x, v)

    def experts_act(act):
        act.wait_ge(nk_ready, 1)

        def split_high(x, v, used=None):
            act.wait_ge(rawm_in[v % RAW], loaded(x.e, v))
            if used is not None:
                act.wait_ge(half_used, used)
            nc.scalar.activation(flat(wh[:, v % SPL, :, :]), flat(rawm[:, v % RAW, :, :]), ACT.Copy).then_inc(wh_done, 1)

        def tokens_high(x):
            def work(b):
                m = min(b, 1)
                act.wait_ge(xt_done[m], x.count(1, 0, b))
                nc.scalar.activation(flat(xh[:, b, :, :]), flat(ps[:, 5:7, :]), ACT.Copy).then_inc(xh_done[m], 1)
            x.blocks(work)

        def sigmoid(x, t):
            def work(b):
                m, s = min(b, 1), (1 + b if b else t % 2)
                act.wait_ge(g_ready[m], x.count(T_GU, t, b))
                nc.scalar.activation(gsu[:, s, 1, :], gsu[:, s, 0, :], ACT.Sigmoid, scale=ALPHA).then_inc(s_done[m], 1)
            x.blocks(work)

        def act_high(x, t):
            def work(b):
                m = min(b, 1)
                act.wait_ge(at_done[m], x.count(T_GU, t, b))
                nc.scalar.activation(flat(ah[:, b, 2 * t:2 * t + 2, :]), ps[:, 7, 0:2 * P], ACT.Copy).then_inc(ah_done[m], 1)
            x.blocks(work)

        def outputs(x, d, after):
            def work(b):
                m = min(b, 1)
                if b:
                    act.wait_ge(acc_more, x.count(U_ALL, T_GU + d, b))
                    act.wait_ge(xt_done[1], after.all_more(1, 0))
                    act.wait_ge(y_out[1], x.stored(1))
                else:
                    act.wait_ge(half_used, x.e * HALVES + (10 + 2 * d))
                    act.wait_ge(y_out[0], x.stored(0))
                dst = xy[b] if b else y0
                nc.scalar.activation(dst[:, d * UN:(d + 1) * UN], ps[:, 1 + b if b else d, :],
                                     ACT.Copy).then_inc(y_copied[1] if b else y_half_copied[d], 1)
            x.blocks(work)

        def middle(x):
            def split(v):
                split_high(x, v, x.e * HALVES + (v - SPL + 1))
            split(4)
            sigmoid(x, 0)
            split(5)
            split(6)
            act_high(x, 0)
            sigmoid(x, 1)
            split(7)
            split(8)
            act_high(x, 1)
            sigmoid(x, 2)
            split(9)
            split(10)
            act_high(x, 2)
            sigmoid(x, 3)
            split(11)
            act_high(x, 3)

        first = Expert(act, 0)
        tokens_high(first)
        for v in range(SPL):
            split_high(first, v)
        with act.Fori(0, E - 1) as e:
            x = Expert(act, e)
            middle(x)
            after = Expert(act, e + 1)
            tokens_high(after)
            split_high(after, 0, e * HALVES + (HALVES - SPL + 1))
            split_high(after, 1, e * HALVES + (HALVES - SPL + 2))
            outputs(x, 0, after)
            split_high(after, 2, e * HALVES + (HALVES - SPL + 3))
            outputs(x, 1, after)
            split_high(after, 3, e * HALVES + (HALVES - SPL + 4))
        last, end = Expert(act, E - 1), Expert(act, E)
        middle(last)
        tokens_high(end)
        outputs(last, 0, end)
        outputs(last, 1, end)

    def experts_dve(dve):
        def split_low(x, v):
            if v in POOL_LOW:
                return
            dve.wait_ge(wh_done, x.e * HALVES + (v + 1))
            nc.vector.tensor_tensor(flat(wl[:, v % SPL, :, :]), flat(rawm[:, v % RAW, :, :]), flat(wh[:, v % SPL, :, :]),
                                    ALU.subtract).then_inc(wl_done, 1)

        def tokens_low(x):
            def work(b):
                m = min(b, 1)
                dve.wait_ge(xh_done[m], x.count(1, 0, b))
                nc.vector.tensor_tensor(flat(xl[:, b, :, :]), flat(ps[:, 5:7, :]), flat(xh[:, b, :, :]),
                                        ALU.subtract).then_inc(xl_done[m], 1)
            x.blocks(work)

        def act_low(x, t, blocks):
            def work(b):
                m = min(b, 1)
                dve.wait_ge(ah_done[m], x.count(T_GU, t, b))
                nc.vector.tensor_tensor(flat(al[:, b, 2 * t:2 * t + 2, :]), ps[:, 7, 0:2 * P],
                                        flat(ah[:, b, 2 * t:2 * t + 2, :]), ALU.subtract).then_inc(al_done[m], 1)
            blocks(work)

        def gate_up(x, t):
            def work(b):
                m, s = min(b, 1), (1 + b if b else t % 2)
                bank = 1 + b if b else t % 2
                if b:
                    dve.wait_ge(acc_more, x.count(U_ALL, t, b))
                    if t:
                        dve.wait_ge(at_done[1], x.count(T_GU, t - 1, b))
                else:
                    dve.wait_ge(half_used, x.e * HALVES + (2 * t + 2))
                nc.vector.tensor_scalar(gsu[:, s, 0, :], ps[:, bank, 0:256], LIMIT, None, ALU.min).then_inc(g_ready[m], 1)
                nc.vector.tensor_scalar(gsu[:, s, 2, :], ps[:, bank, 256:512], LIMIT, -LIMIT, ALU.min,
                                        ALU.max).then_inc(acc_free[m], 1)
                dve.wait_ge(g_ready[m], x.count(T_GU, t, b))
                dve.wait_ge(acc_free[m], x.count(T_GU, t, b))
                nc.vector.scalar_tensor_tensor(gsu[:, s, 2, :], gsu[:, s, 2, :], 1.0, gsu[:, s, 0, :], ALU.add,
                                               ALU.mult).then_inc(up_ready[m], 1)
            x.blocks(work)

        def at_once(work):
            work(0)

        dve.wait_ge(nk_ready, 1)
        tokens_low(Expert(dve, 0))
        with dve.Fori(0, E) as e:
            x = Expert(dve, e)
            for v in range(4):
                split_low(x, v)
            gate_up(x, 0)
            split_low(x, 4)
            split_low(x, 5)
            act_low(x, 0, x.further)
            gate_up(x, 1)
            act_low(x, 0, at_once)
            split_low(x, 6)
            split_low(x, 7)
            act_low(x, 1, x.further)
            gate_up(x, 2)
            act_low(x, 1, at_once)
            split_low(x, 8)
            split_low(x, 9)
            act_low(x, 2, x.further)
            gate_up(x, 3)
            act_low(x, 2, at_once)
            split_low(x, 10)
            act_low(x, 3, x.blocks)
            split_low(x, 11)
            tokens_low(Expert(dve, e + 1))

    def experts_pool(pool):
        pool.wait_ge(h2_ready, TC)
        pool.wait_ge(lg_ready, TC)
        nc.gpsimd.memset(xg0[:], 0.0).then_inc(pool_set, 1)
        for b in range(1, NB):
            nc.gpsimd.memset(xy[b][:], 0.0).then_inc(pool_set, 1)
        pool.wait_ge(pool_set, 3 + NB)
        pool.wait_ge(tab_done, 1)
        pool.wait_ge(nk_ready, 1)
        for w in range(2):
            pool.wait_ge(h2_out[w], 32)

        def gather(x, done):
            def work(b):
                m = min(b, 1)
                if b:
                    pool.wait_ge(xt_done[1], x.earlier(1, 1))
                    pool.wait_ge(y_out[1], done.stored(1))
                else:
                    pool.wait_ge(xt_done[0], x.earlier(1, 0))
                pool.sem_inc(pool_passed, 1)
                nc.gpsimd.tensor_copy(icur[:, 0, b:b + 1], gtab[:, b, bass.ds(x.e + 1, 1)]).then_inc(gcur[m], 1)
                pool.wait_ge(gcur[m], x.count(1, 0, b))
                pool.sem_inc(pool_passed, 1)
                pool.indirect_dma_start(out=(xy[b] if b else xg0)[:], out_offset=None, in_=h2_d,
                                        in_offset=bass.IndirectOffsetOnAxis(ap=icur[:, 0, b:b + 1], axis=0),
                                        bounds_check=T - 1, oob_is_err=False).then_inc(xg_in[m], 16)
            x.blocks(work)

        def scatter(x):
            def work(b):
                m = min(b, 1)
                if b:
                    pool.wait_ge(y_copied[1], x.all_more(2, 1))
                    pool.wait_ge(y_out[1], x.stored(1))
                else:
                    for half in y_half_copied:
                        pool.wait_ge(half, x.count(1, 0, 0))
                    pool.wait_ge(y_out[0], x.stored(0))
                pool.sem_inc(pool_passed, 1)
                nc.gpsimd.tensor_copy(icur[:, 1, b:b + 1], stab[:, b, bass.ds(x.e + 1, 1)]).then_inc(scur[m], 1)
                pool.wait_ge(scur[m], x.count(1, 0, b))
                pool.sem_inc(pool_passed, 1)
                pool.indirect_dma_start(out=y_d, out_offset=bass.IndirectOffsetOnAxis(ap=icur[:, 1, b:b + 1], axis=0),
                                        in_=(xy[b] if b else y0)[:], in_offset=None, bounds_check=T * TOPK - 1,
                                        oob_is_err=False).then_inc(y_out[m], 16)
            x.blocks(work)

        def activation(x, t):
            def work(b):
                m, s = min(b, 1), (1 + b if b else t % 2)
                pool.wait_ge(s_done[m], x.count(T_GU, t, b))
                pool.wait_ge(up_ready[m], x.count(T_GU, t, b))
                nc.gpsimd.tensor_tensor(gsu[:, s, 2, :], gsu[:, s, 2, :], gsu[:, s, 1, :], ALU.mult).then_inc(act_ready[m], 1)
            x.blocks(work)

        def split_low(x, v):
            pool.wait_ge(wh_done, x.e * HALVES + (v + 1))
            nc.gpsimd.tensor_tensor(flat(wl[:, v % SPL, :, :]), flat(rawm[:, v % RAW, :, :]), flat(wh[:, v % SPL, :, :]),
                                    ALU.subtract).then_inc(wl_pool_done, 1)

        first = Expert(pool, 0)
        gather(first, first)
        with pool.Fori(0, E) as e:
            x = Expert(pool, e)
            gather(Expert(pool, e + 1), x)
            for t in range(T_GU):
                activation(x, t)
                for v in POOL_LOW:
                    if v == max(2 * t + 5, 0):
                        split_low(x, v)
            scatter(x)

    fin_out = [sem("fin_out0"), sem("fin_out1")]
    yt_in, x1e_in = [sem("yt_in0"), sem("yt_in1")], [sem("x1e_in0"), sem("x1e_in1")]
    comb_step, fsq_ready, frs_step, fg_ready, fin_ready = map(
        sem, ("comb_step", "fsq_ready", "frs_step", "fg_ready", "fin_ready"))

    def final_pool(pool, power):
        end = Expert(pool, E)
        pool.wait_ge(y_out[0], 16 * (E + START))
        pool.wait_ge(y_out[1], end.stored(1))
        pool.sem_inc(pool_passed, 1)
        rows_of = y_d.rearrange("(t p j) d -> t p j d", p=P, j=TOPK)
        for t in range(TC):
            w = t % 2
            if t >= 2:
                pool.wait_ge(fin_ready, t - 1)
            pool.dma_start(yt[:, w, :, :], rows_of[t]).then_inc(yt_in[w], 16)
            pool.dma_start(x1e[:, w, :], x1_d[t * P:(t + 1) * P, :]).then_inc(x1e_in[w], 16)
            if t:
                power(rs1[:, 2, t - 1:t], rs1[:, 1, t - 1:t], frs_step, 2 * t - 1)
        power(rs1[:, 2, TC - 1:TC], rs1[:, 1, TC - 1:TC], frs_step, 2 * TC - 1)

    def final_dve(dve):
        for t in range(TC):
            w = t % 2
            dve.wait_ge(yt_in[w], 16 * (t // 2 + 1))
            for j in range(TOPK):
                wgt = topw[:, t * TOPK + j:t * TOPK + j + 1]
                if j == 0:
                    ins = nc.vector.tensor_scalar(yo[:, w, :], yt[:, w, j, :], wgt, None, ALU.mult)
                else:
                    dve.wait_ge(comb_step, t * TOPK + j)
                    ins = nc.vector.scalar_tensor_tensor(yo[:, w, :], yt[:, w, j, :], wgt, yo[:, w, :], ALU.mult, ALU.add)
                ins.then_inc(comb_step, 1)
            dve.wait_ge(fsq_ready, t + 1)
            nc.vector.tensor_scalar(rs1[:, 1, t:t + 1], rs1[:, 0, t:t + 1], 1.0 / D, EPS, ALU.mult,
                                    ALU.add).then_inc(frs_step, 1)
            dve.wait_ge(frs_step, 2 * t + 2)
            dve.wait_ge(comb_step, (t + 1) * TOPK)
            nc.vector.scalar_tensor_tensor(yo[:, w, :], yo[:, w, :], rs1[:, 2, t:t + 1], gpf[:], ALU.mult,
                                           ALU.mult).then_inc(fg_ready, 1)
            dve.wait_ge(fg_ready, t + 1)
            dve.wait_ge(x1e_in[w], 16 * (t // 2 + 1))
            if t >= 2:
                dve.wait_ge(fin_out[w], 16)
            nc.vector.tensor_tensor(fin[:, w, :], x1e[:, w, :], yo[:, w, :], ALU.add).then_inc(fin_ready, 1)

    def final_act(act):
        for t in range(TC):
            act.wait_ge(comb_step, (t + 1) * TOPK)
            if t:
                act.wait_ge(fsq_ready, t)
            nc.scalar.activation(junke[:], yo[:, t % 2, :], ACT.Square, accum_out=rs1[:, 0, t:t + 1]).then_inc(fsq_ready, 1)

    def final_sync(sp):
        for t in range(TC):
            w = t % 2
            sp.wait_ge(fin_ready, t + 1)
            sp.dma_start(out[0, t * P:(t + 1) * P, :], fin[:, w, :]).then_inc(fin_out[w], 16)
        for w in range(2):
            sp.wait_ge(fin_out[w], 32)
    block = ctx.enter_context(nc.Block())

    @block.sync
    def _(sp):
        def load(slot, g, src, n=UN):
            if not isinstance(g, int) or g >= 4:
                sp.wait_ge(raw_used, g - 3)
            sp.dma_start(raw[:, slot, :, 0:n], src).then_inc(raw_in[slot], 16)

        def ada(col, h):
            return w_ada[0, h * HK * P:(h + 1) * HK * P, col].rearrange("(k p) n -> p k n", p=P)

        for g in range(8):
            load(g % 4, g, ada(bass.ds(g // 2 * UN, UN), g % 2))
        load(0, 8, win_half(bass.ds(C_KA, 256), 0), 256)
        load(1, 9, win_half(bass.ds(C_KA, 256), 1), 256)
        load(2, 10, win_half(bass.ds(C_QA, UN), 0))
        load(3, 11, win_half(bass.ds(C_QA, UN), 1))
        load(0, 12, ada(bass.ds(4 * UN, UN), 0))
        load(1, 13, win_half(bass.ds(C_QB, UN), 0))
        load(2, 14, ada(bass.ds(4 * UN, UN), 1))
        with sp.Fori(1, N_W - 1) as u:
            load(3, 11 + 4 * u, win_half(bass.ds(C_QB + (u - 1) * UN, UN), 1))
            load(0, 12 + 4 * u, ada(bass.ds((4 + u) * UN, UN), 0))
            load(1, 13 + 4 * u, win_half(bass.ds(C_QB + u * UN, UN), 0))
            load(2, 14 + 4 * u, ada(bass.ds((4 + u) * UN, UN), 1))
        g = 11 + 4 * (N_W - 1)
        load(3, g, win_half(bass.ds(C_QB + (N_W - 2) * UN, UN), 1))
        load(0, g + 1, ada(bass.ds(11 * UN, UN), 0))
        load(1, g + 2, ada(bass.ds(11 * UN, UN), 1))
        sp.wait_ge(acc_done, 5 + 4 * N_W)
        for k in range(2):
            sp.dma_start(wo[:, 4 * k:4 * k + 4, :],
                         w_out[0, 4 * k * P:4 * (k + 1) * P, :].rearrange("(k p) n -> p k n", p=P)).then_inc(wo_in, 16)
        merge_sync(sp)
        experts_sync(sp)
        final_sync(sp)

    @block.scalar
    def _(act):
        act.dma_start(ccol[:], c[0, :].rearrange("(k p) -> p k", p=P), allow_slow_non_contiguous=True).then_inc(c_in, 16)
        act.dma_start(bmods[:], b_ada[0:1, 0:4 * UN]).then_inc(bmods_in, 16)
        act.dma_start(xs[:], x[0].rearrange("(c p) d -> p c d", p=P)).then_inc(x_in, 16)
        act.dma_start(gprec[:], g_mix_pre[0].rearrange("(k p) -> p k", p=P),
                      allow_slow_non_contiguous=True).then_inc(gpre_in, 16)
        act.wait_ge(c_in, 16)
        nc.scalar.activation(csig[:], ccol[:], ACT.Sigmoid).then_inc(csig_ready, 1)
        act.wait_ge(lam_step, 2)
        nc.scalar.activation(lexp[:], lsum[:], ACT.Exp).then_inc(lexp_ready, 1)
        act.wait_ge(x_in, 16)
        for t in range(TC):
            if t:
                act.wait_ge(xss_ready, t)
            nc.scalar.activation(xsq[:], xs[:, t, :], ACT.Square, accum_out=rs[:, 0, t:t + 1]).then_inc(xss_ready, 1)
        for t in range(TC):
            act.wait_ge(ht_ps, t + 1)
            b = 4 + 2 * (t % 2)
            nc.scalar.activation(ht[:, :, t * P:(t + 1) * P], ps[:, b:b + 2, :].rearrange("p a (b c) -> p (a b) c", c=P),
                                 ACT.Copy).then_inc(ht_copied, 1)
        for j in range(4):
            act.wait_ge(raw_used, 2 * j + 2)
            nc.scalar.activation(mrow[:, j, :], ps[0:1, j, :], ACT.Copy).then_inc(mrow_ready, 1)

        def split_high(m, slot, m_slot, arrivals, n=UN):
            act.wait_ge(raw_in[slot], 16 * arrivals)
            nc.scalar.activation(whf[:, m_slot, :, 0:n], raw[:, slot, :, 0:n], ACT.Copy).then_inc(wh_ready, 1)

        split_high(0, 0, 0, 3, 256)
        for k in range(KC):
            act.wait_ge(h_ready, k + 1)
            nc.scalar.activation(hh[:, k, :], ht[:, k, :], ACT.Copy).then_inc(hh_ready, 1)
        split_high(1, 1, 1, 3, 256)
        act.wait_ge(half0_used, 1)
        split_high(2, 2, 0, 3)
        act.wait_ge(acc_done, 1)
        for g in range(KV_A):
            for half in range(2):
                nc.scalar.activation(ka2[64 * half:64 * half + 64, g, :], ps[64 * g:64 * g + 64, 4, :],
                                     ACT.Copy).then_inc(evac_done, 1)
        for t in range(TC):
            act.wait_ge(acc_done, 2 + t)
            nc.scalar.activation(va[:, t, :], ps[:, t, 0:P], ACT.Copy).then_inc(evac_done, 1)

        def unit(u, dst, last=False):
            act.wait_ge(acc_done, 5 + 4 * u)
            split_high(3 + 2 * u, 3, 1, 3 + u)
            if not last:
                act.wait_ge(half0_used, 2 + u)
                split_high(4 + 2 * u, 1, 0, 4 + u)
            for k in range(4):
                act.wait_ge(acc_done, 5 + 4 * u + k + 1)
                nc.scalar.activation(dst(u, k), ps[:, k, :], ACT.Copy).then_inc(evac_done, 1)

        def to_qk(u, k):
            return qk[:, bass.ds(4 * u + k, 1), :].rearrange("p a n -> p (a n)")

        def to_nat(u, k):
            return nat[:, k, bass.ds((u - N_T) * UN, UN)]

        with act.Fori(0, N_T) as u:
            unit(u, to_qk)
        with act.Fori(N_T, N_W - 1) as u:
            unit(u, to_nat)
        act.wait_ge(latemod_ps, 2)
        nc.scalar.activation(shf[:], flat(ps[:, 6:8, :]), ACT.Copy).then_inc(shf_ready, 1)
        unit(N_W - 1, to_nat, last=True)
        attention_act(act)
        merge_act(act)
        experts_act(act)
        final_act(act)


    @block.tensor
    def _(pe):
        on_all = one[:, 0:1].to_broadcast([P, P])
        accf = acc[:].rearrange("p a b -> p (a b)")

        def spread(j, bank, signal=None):
            ins = nc.tensor.matmul(ps[:, bank, :], on_all, accf[:, j * UN:(j + 1) * UN], start=True, stop=True)
            if signal is not None:
                ins.then_inc(signal, 1)

        for s in from_one:
            pe.sem_inc(s, START)
        def first_mods(j):
            for h in range(2):
                g = 2 * j + h
                pe.wait_ge(raw_in[g % 4], 16 * (g // 4 + 1))
                for k in range(HK):
                    ins = nc.tensor.matmul(ps[0:1, j, :], cact[:, HK * h + k:HK * h + k + 1], raw[:, g % 4, k, :],
                                           start=h == 0 and k == 0, stop=False)
                if h == 0:
                    ins.then_inc(raw_used, 1)
            nc.tensor.matmul(ps[0:1, j, :], one[0:1, 0:1], bmods[:, j * UN:(j + 1) * UN], start=False, stop=True).then_inc(raw_used, 1)

        pe.wait_ge(cact_ready, 1)
        pe.wait_ge(one_set, 1)
        pe.wait_ge(bmods_in, 16)
        first_mods(0)
        first_mods(1)
        pe.wait_ge(small_in, 16 * N_SMALL)
        for t in range(TC):
            pe.wait_ge(hx_ready, t + 1)
            if t >= 2:
                pe.wait_ge(ht_copied, t - 1)
            for k in range(KC):
                ins = nc.tensor.transpose(ps[:, 4 + 2 * (t % 2) + k // 4, (k % 4) * P:(k % 4 + 1) * P],
                                          hx[:, t % 2, k * P:(k + 1) * P], ident[:])
            ins.then_inc(ht_ps, 1)
        first_mods(2)
        first_mods(3)
        pe.wait_ge(ht_copied, TC)
        for j in range(4):
            pe.wait_ge(mrow_ready, j + 1)
            for q in range(4):
                ins = nc.tensor.matmul(ps[:, 4, 4 * j + q:4 * j + q + 1], mrow[0:1, j, q * P:(q + 1) * P], one[0:1, 0:1],
                                       start=True, stop=True)
        ins.then_inc(col_ps, 1)

        def three(dst, a_h, a_l, b_h, b_l, first, last):
            nc.tensor.matmul(dst, a_h, b_h, start=first, stop=False)
            nc.tensor.matmul(dst, a_h, b_l, start=False, stop=False)
            return nc.tensor.matmul(dst, a_l, b_h, start=False, stop=last)

        for h in range(2):
            pe.wait_ge(raw_used, 9 + h)
            for k in range(HK):
                kk = HK * h + k
                pe.wait_ge(hl_ready, kk + 1)
                ins = three(ps[:, 4, :], whf[:, h, k, 0:P], wlf[:, h, k, 0:P], hh[:, kk, :], hl[:, kk, :],
                            kk == 0, kk == KC - 1)
            if h:
                ins.then_inc(acc_done, 1)
            else:
                pe.wait_ge(mrow_ready, 4)
            for t in range(TC):
                for k in range(HK):
                    kk = HK * h + k
                    ins = three(ps[:, t, 0:P], hh[:, kk, t * P:(t + 1) * P], hl[:, kk, t * P:(t + 1) * P],
                                whf[:, h, k, P:2 * P], wlf[:, h, k, P:2 * P], kk == 0, kk == KC - 1)
                if h:
                    ins.then_inc(acc_done, 1)
            if h == 0:
                ins.then_inc(half0_used, 1)
        pe.wait_ge(tab_ready, 1)
        pe.wait_ge(oh_in, 16)
        nc.tensor.matmul(ps[0:H_A, 6, 0:REL], tabx[:, 0:H_A], oh[:, 0:REL], start=True, stop=True).then_inc(rv_ps, 1)
        nc.tensor.matmul(ps[0:H_B, 7, 0:REL], tabx[:, H_A:H_A + H_B], oh[:, REL:2 * REL], start=True,
                         stop=True).then_inc(rv_ps, 1)

        def unit(u, transposed):
            for h in range(2):
                pe.wait_ge(raw_used, (10 if h == 0 else 12) + 4 * u)
                for q in range(4):
                    if h == 0:
                        pe.wait_ge(evac_done, 5 + 4 * u + q)
                    for k in range(HK):
                        kk = HK * h + k
                        if transposed:
                            ins = three(ps[:, q, :], whf[:, h, k, q * P:(q + 1) * P], wlf[:, h, k, q * P:(q + 1) * P],
                                        hh[:, kk, :], hl[:, kk, :], kk == 0, kk == KC - 1)
                        else:
                            ins = three(ps[:, q, :], hh[:, kk, q * P:(q + 1) * P], hl[:, kk, q * P:(q + 1) * P],
                                        whf[:, h, k, :], wlf[:, h, k, :], kk == 0, kk == KC - 1)
                    if h:
                        ins.then_inc(acc_done, 1)
                if h == 0:
                    ins.then_inc(half0_used, 1)

        pe.wait_ge(raw_used, 11)
        with pe.Fori(0, N_T) as u:
            unit(u, True)
        with pe.Fori(N_T, N_W - 1) as u:
            unit(u, False)
        pe.wait_ge(raw_used, 27)
        pe.wait_ge(rv_ready, 2)
        for j in range(4, 8):
            spread(j, j, latemod_ps if j % 2 else None)
        unit(N_W - 1, False)
        pe.wait_ge(raw_used, 42)
        pe.wait_ge(latemod_ready, 1)
        pe.wait_ge(shf_ready, 1)
        for j in range(8, 12):
            spread(j, j - 4, latemod_ps if j % 2 else None)
        pe.wait_ge(evac_done, 8 + 4 * N_W)
        attention_pe(pe)
        merge_pe(pe)
        experts_pe(pe)

    @block.vector
    def _(dve):
        accf = acc[:].rearrange("p a b -> p (a b)")
        nc.vector.memset(one[:], 1.0).then_inc(one_set, 1)
        nc.vector.memset(nhalf[:], -0.5).then_inc(one_set, 1)
        nc.vector.memset(tabx[N_BUCKETS:N_BUCKETS + 1, :], MASKED).then_inc(tab_ready, 1)
        dve.wait_ge(c_in, 16)
        dve.wait_ge(csig_ready, 1)
        nc.vector.tensor_tensor(cact[:], ccol[:], csig[:], ALU.mult).then_inc(cact_ready, 1)
        dve.wait_ge(small_in, 16 * N_SMALL)
        nc.vector.tensor_tensor(lprod[:], lp[:, 0::2, :], lp[:, 1::2, :], ALU.mult).then_inc(lam_step, 1)
        dve.wait_ge(lam_step, 1)
        nc.vector.tensor_reduce(lsum[:], lprod[:], AX_X, ALU.add).then_inc(lam_step, 1)
        nc.vector.tensor_scalar(subgs[:], subg[:], 1.0 - LAM_INIT, None, ALU.mult).then_inc(lam_step, 1)
        nc.vector.tensor_scalar(nsink[:], sinkb[:], -1.0, None, ALU.mult).then_inc(lam_step, 1)
        dve.wait_ge(lexp_ready, 1)
        nc.vector.tensor_scalar(nlam0[:], lexp[:, 1:2], -LAM_INIT, None, ALU.add).then_inc(lam_step, 1)
        dve.wait_ge(lam_step, 5)
        nc.vector.tensor_tensor(nlam[:], nlam0[:], lexp[:, 0:1], ALU.subtract).then_inc(lam_step, 1)
        dve.wait_ge(bada_in, 16)
        dve.wait_ge(cact_ready, 1)

        def ada(a, h, slot, arrivals, g, last_g):
            dve.wait_ge(raw_in[slot], 16 * arrivals)
            dst = accf[:, bass.ds(a * UN, UN)]
            for k in range(HK):
                if k == 0 and h:
                    dve.wait_ge(raw_used, last_g + 1)
                elif k:
                    dve.wait_ge(ada_step, 3 * (2 * (a - 4) + h) + k)
                ins = nc.vector.scalar_tensor_tensor(dst, raw[:, slot, k, :], cact[:, HK * h + k:HK * h + k + 1], dst,
                                                     ALU.mult, ALU.add)
                ins.then_inc(raw_used if k == HK - 1 else ada_step, 1)

        dve.wait_ge(xss_ready, TC)
        nc.vector.tensor_scalar(rs[:, 1, :], rs[:, 0, :], 1.0 / D, EPS, ALU.mult, ALU.add).then_inc(xrs_step, 1)
        dve.wait_ge(xrs_step, 2)
        dve.wait_ge(x_in, 16)
        for t in range(TC):
            if t >= 2:
                dve.wait_ge(ht_ps, t - 1)
            nc.vector.tensor_scalar(hx[:, t % 2, :], xs[:, t, :], rs[:, 2, t:t + 1], None, ALU.mult).then_inc(hx_ready, 1)

        def split_low(m, slot, m_slot, n=UN):
            dve.wait_ge(wh_ready, m + 1)
            nc.vector.tensor_tensor(wlf[:, m_slot, :, 0:n], raw[:, slot, :, 0:n], whf[:, m_slot, :, 0:n],
                                    ALU.subtract).then_inc(raw_used, 1)

        dve.wait_ge(raw_used, 8)
        split_low(0, 0, 0, 256)
        dve.wait_ge(gpre_in, 16)
        dve.wait_ge(col_ps, 1)
        nc.vector.tensor_copy(shcol[:], ps[:, 4, 0:KC]).then_inc(col_ready, 1)
        nc.vector.scalar_tensor_tensor(gcol[:], ps[:, 4, KC:2 * KC], 1.0, gprec[:], ALU.add, ALU.mult).then_inc(col_ready, 1)
        dve.wait_ge(col_ready, 2)
        dve.wait_ge(ht_copied, TC)

        def h_low(k):
            dve.wait_ge(hh_ready, k + 1)
            nc.vector.tensor_tensor(hl[:, k, :], ht[:, k, :], hh[:, k, :], ALU.subtract).then_inc(hl_ready, 1)

        for k in range(KC):
            nc.vector.tensor_scalar(ht[:, k, :], ht[:, k, :], gcol[:, k:k + 1], shcol[:, k:k + 1], ALU.mult,
                                    ALU.add).then_inc(h_ready, 1)
            if k:
                h_low(k - 1)
        h_low(KC - 1)
        split_low(1, 1, 1, 256)
        split_low(2, 2, 0)
        for b in range(2):
            n = (H_A, H_B)[b]
            dve.wait_ge(rv_ps, b + 1)
            nc.vector.tensor_copy(rv[0:n, b, :], ps[0:n, 6 + b, 0:REL]).then_inc(rv_ready, 1)

        def unit(u, last=False):
            split_low(3 + 2 * u, 3, 1)
            ada(4 + u, 0, 0, 4 + u, 12 + 4 * u, None)
            if not last:
                split_low(4 + 2 * u, 1, 0)
                ada(4 + u, 1, 2, 4 + u, 14 + 4 * u, 12 + 4 * u)
            else:
                ada(4 + u, 1, 1, 4 + u, 13 + 4 * u, 12 + 4 * u)

        with dve.Fori(0, N_W - 1) as u:
            unit(u)
        dve.wait_ge(grow_in, 32)
        dve.wait_ge(latemod_ps, 1)
        nc.vector.tensor_tensor(halves(gpm[:]), ps[:, 4:6, :], halves(grow1[:]), ALU.mult).then_inc(latemod_ready, 1)
        unit(N_W - 1, last=True)
        dve.wait_ge(latemod_ps, 3)
        nc.vector.scalar_tensor_tensor(halves(gf[:]), ps[:, 4:6, :], 1.0, halves(grow2[:]), ALU.add,
                                       ALU.mult).then_inc(latemod_ready, 1)
        attention_dve(dve)
        merge_dve(dve)
        experts_dve(dve)
        final_dve(dve)

    @block.gpsimd
    def _(pool):
        nc.gpsimd.memset(acc[:], 0.0).then_inc(pool_set, 1)
        pool.dma_start(ident[:], ident_c).then_inc(small_in, 16)
        pool.dma_start(tabx[0:N_BUCKETS, :], rel_bias_table).then_inc(small_in, 16)
        for g in range(KV_A):
            for a in range(2):
                src = bass.AP(tensor=attn_sinks.tensor, offset=attn_sinks.offset + 4 * g + a, ap=[[0, P], [2, 2]])
                pool.dma_start(sinkb[:, 4 * g + 2 * a:4 * g + 2 * a + 2], src, allow_slow_non_contiguous=True).then_inc(small_in, 16)
        pool.dma_start(farb[:], bcast(rel_bias_table[N_BUCKETS - 1, H_A:H_A + H_B], H_B)).then_inc(small_in, 16)
        pool.dma_start(subg[:], diff_subln_g[0].rearrange("(p a) -> p a", a=1)).then_inc(small_in, 16)
        pool.dma_start(lp[:].rearrange("p a b -> p (a b)"),
                       bcast(diff_lambda[0].rearrange("a b -> (a b)"), 4 * DH)).then_inc(small_in, 16)
        pool.wait_ge(pool_set, 1)
        pool.dma_start(acc[0:1, :, :].rearrange("p a b -> p (a b)"), b_ada).then_inc(bada_in, 16)

        def power(dst, src, done, n):
            pool.wait_ge(done, n)
            nc.gpsimd.tensor_tensor(dst, src, nhalf[:, 0:src.shape[1]], ALU.pow).then_inc(done, 1)

        pool.wait_ge(one_set, 2)
        power(rs[:, 2, :], rs[:, 1, :], xrs_step, 1)
        pool.wait_ge(raw_used, 8)
        pool.dma_start(grow1[:], bcast(g_mix_post[0], D)).then_inc(grow_in, 16)
        pool.dma_start(grow2[:], bcast(g_ffn_pre[0], D)).then_inc(grow_in, 16)
        pool.wait_ge(hx_ready, TC)
        pool.dma_start(oh[:], oh_c).then_inc(oh_in, 16)
        pool.wait_ge(rv_ready, 2)
        pool.dma_start(bias_d[0:H_A, :], rv[:, 0, :]).then_inc(biasv_out, 16)
        pool.dma_start(bias_d[H_A:H_A + H_B, :], rv[0:H_B, 1, :]).then_inc(biasv_out, 16)
        pool.wait_ge(biasv_out, 32)
        pool.dma_start(wide_d, bass.AP(tensor=bias_d.tensor, offset=bias_d.offset,
                                       ap=[[REL, H_A + H_B], [0, P], [1, REL]])).then_inc(wide_out, 16)
        pool.wait_ge(wide_out, 16)

        def shifted(head, step, n):
            return bass.AP(tensor=wide_d.tensor, offset=wide_d.offset + head * P * REL + P - 1,
                           ap=[[REL - 1, P], [step * P * REL, n], [1, 2 * P]])

        for g in range(KV_A):
            for a in range(2):
                pool.dma_start(toep[:, 4 * g + 2 * a:4 * g + 2 * a + 2, :],
                               shifted(4 * g + a, 2, 2)).then_inc(toep_in, 16)
        pool.dma_start(toep[:, H_A:H_A + H_B, :], shifted(H_A, 1, H_B)).then_inc(toep_in, 16)
        pool.wait_ge(acc_done, 5 + 4 * N_W)
        pool.dma_start(grow3[:], bcast(g_ffn_post[0], D)).then_inc(grow_in, 16)
        for b in range(3):
            pool.dma_start(ball[32 * b:32 * b + 32, 0:2 * D], b_gate_up[0]).then_inc(ball_in, 16)
            pool.dma_start(ball[32 * b:32 * b + 32, 2 * D:3 * D], b_down[0]).then_inc(ball_in, 16)
        attention_pool(pool, power)
        merge_pool(pool, power)
        experts_pool(pool)
        final_pool(pool, power)


_INS = ['x', 'c', 'rel_bias_table', 'w_ada', 'b_ada', 'g_mix_pre', 'g_mix_post', 'g_ffn_pre', 'g_ffn_post', 'w_in',
        'w_out', 'attn_sinks', 'diff_lambda', 'diff_subln_g', 'w_router', 'b_router', 'w_gate_up', 'b_gate_up',
        'w_down', 'b_down']


def kernel(**inputs):
    import numpy as _np
    import concourse.bacc as _bacc
    from concourse import mybir as _mybir
    from concourse.bass_utils import run_bass_kernel_spmd as _run

    nc = _bacc.Bacc("TRN2", target_bir_lowering=False, num_devices=1)
    arrays, args = {}, []
    for name in _INS:
        a = _np.ascontiguousarray(inputs[name])
        arrays[f"in_{name}"] = a
        args.append(nc.dram_tensor(f"in_{name}", a.shape, _mybir.dt.from_np(a.dtype), kind="ExternalInput").ap())
    out = nc.dram_tensor("out_0", (1, T, D), F32, kind="ExternalOutput").ap()
    build(nc, *args, out)
    r = _run(nc, [arrays], core_ids=[0])
    return r.results[0]["out_0"]
```
